# Optimizing a Trainium2 kernel written in Bass

```python
import math
import jax, jax.numpy as jnp
from jax import lax
import numpy as np

D_MODEL = 1024
BATCH = 1
SEQ = 1024
DEPTH = 1

CHUNK = 64
EPS = 1e-6

SSM_HEADS = 16
SSM_HEAD_DIM = 64
SSM_D_INNER = SSM_HEADS * SSM_HEAD_DIM
SSM_GROUPS = 2
SSM_STATE = 128
SSM_CONV = 4
SSM_XBC = SSM_D_INNER + 2 * SSM_GROUPS * SSM_STATE

GDN_HEADS = 8
GDN_DK = 128
GDN_DV = 128
GDN_KEY = GDN_HEADS * GDN_DK
GDN_VAL = GDN_HEADS * GDN_DV
GDN_CONV = 4
GDN_QKV = 2 * GDN_KEY + GDN_VAL

D_FF = 4 * D_MODEL
FFN_CONV = 3

PLE_DIM = 256

IN_SIZES = (SSM_D_INNER, SSM_XBC, SSM_HEADS, GDN_QKV, GDN_VAL, GDN_HEADS, GDN_HEADS, 2 * D_MODEL)
IN_SPLITS = tuple(sum(IN_SIZES[:j + 1]) for j in range(len(IN_SIZES) - 1))
D_IN = sum(IN_SIZES)

kernel_name = 'hybrid_ssd_deltanet_parallel_gated_block'

def rms_norm(x, g):
    xf = x.astype(jnp.float32)
    y = xf * lax.rsqrt(jnp.mean(xf * xf, axis=-1, keepdims=True) + EPS)
    return (y * g.astype(jnp.float32)).astype(x.dtype)

def causal_dwconv(x, w):
    k, c = w.shape
    return lax.conv_general_dilated(
        x, w[:, None, :].astype(x.dtype), window_strides=(1,), padding=[(k - 1, 0)],
        dimension_numbers=('NWC', 'WIO', 'NWC'), feature_group_count=c)

def l2_normalize(x):
    return x * lax.rsqrt(jnp.sum(x * x, axis=-1, keepdims=True) + EPS)

def ssd_chunked(xh, dt, a, bm, cm):
    bsz, s, h, pd = xh.shape
    g, n = bm.shape[2], bm.shape[3]
    r = h // g
    c = s // CHUNK
    xc = (xh * dt[..., None]).reshape(bsz, c, CHUNK, g, r, pd)
    a_dt = jnp.moveaxis((dt * a).reshape(bsz, c, CHUNK, g, r), 2, -1)
    a_cum = jnp.cumsum(a_dt, axis=-1)
    bc = bm.reshape(bsz, c, CHUNK, g, n)
    cc = cm.reshape(bsz, c, CHUNK, g, n)
    causal = jnp.tril(jnp.ones((CHUNK, CHUNK), dtype=bool))
    seg = a_cum[..., :, None] - a_cum[..., None, :]
    lmat = jnp.exp(jnp.where(causal, seg, -jnp.inf))
    scores = jnp.einsum('bclgn,bcsgn->bcgls', cc, bc)
    y_diag = jnp.einsum('bcgrls,bcsgrp->bclgrp', scores[:, :, :, None] * lmat, xc)
    decay_states = jnp.exp(a_cum[..., -1:] - a_cum)
    states = jnp.einsum('bclgn,bcgrl,bclgrp->bcgrpn', bc, decay_states, xc)
    chunk_decay = jnp.exp(a_cum[..., -1])

    def step(carry, inp):
        st, dec = inp
        return carry * dec[..., None, None] + st, carry

    init = jnp.zeros((bsz, g, r, pd, n), jnp.float32)
    _, prev = lax.scan(step, init, (jnp.moveaxis(states, 1, 0), jnp.moveaxis(chunk_decay, 1, 0)))
    prev = jnp.moveaxis(prev, 0, 1)
    y_off = jnp.einsum('bclgn,bcgrpn,bcgrl->bclgrp', cc, prev, jnp.exp(a_cum))
    return (y_diag + y_off).reshape(bsz, s, h, pd)

def mamba2_branch(z, xbc, dt_raw, conv_w, conv_b, dt_bias, a_log, d_skip, norm_g):
    dtype = z.dtype
    xbc = jax.nn.silu(causal_dwconv(xbc, conv_w) + conv_b)
    xs, bm, cm = jnp.split(xbc, [SSM_D_INNER, SSM_D_INNER + SSM_GROUPS * SSM_STATE], axis=-1)
    bsz, s, _ = xs.shape
    f32 = jnp.float32
    xh = xs.reshape(bsz, s, SSM_HEADS, SSM_HEAD_DIM).astype(f32)
    dt = jax.nn.softplus(dt_raw.astype(f32) + dt_bias.astype(f32))
    a = -jnp.exp(a_log.astype(f32))
    y = ssd_chunked(xh, dt, a,
                    bm.reshape(bsz, s, SSM_GROUPS, SSM_STATE).astype(f32),
                    cm.reshape(bsz, s, SSM_GROUPS, SSM_STATE).astype(f32))
    y = y + d_skip.astype(f32)[:, None] * xh
    y = y.reshape(bsz, s, SSM_D_INNER) * jax.nn.silu(z.astype(f32))
    yg = y.reshape(bsz, s, SSM_GROUPS, SSM_D_INNER // SSM_GROUPS)
    yg = yg * lax.rsqrt(jnp.mean(yg * yg, axis=-1, keepdims=True) + EPS)
    return (yg.reshape(bsz, s, SSM_D_INNER) * norm_g.astype(f32)).astype(dtype)

def gated_delta_chunked(q, k, v, g, beta):
    bsz, s, h, dk = q.shape
    dv = v.shape[-1]
    c = s // CHUNK

    def chunks(t):
        return jnp.moveaxis(t.reshape((bsz, c, CHUNK) + t.shape[2:]), 3, 2)

    q = chunks(q) * (dk ** -0.5)
    k = chunks(k)
    v = chunks(v)
    g = chunks(g)
    beta = chunks(beta)
    gc = jnp.cumsum(g, axis=-1)
    lower = jnp.tril(jnp.ones((CHUNK, CHUNK), dtype=bool))
    strict = jnp.tril(jnp.ones((CHUNK, CHUNK), jnp.float32), -1)
    decay = jnp.exp(jnp.where(lower, gc[..., :, None] - gc[..., None, :], -jnp.inf))
    kb = k * beta[..., None]
    a_mat = jnp.einsum('bchid,bchjd->bchij', kb, k) * decay * strict
    t_mat = a_mat + jnp.eye(CHUNK, dtype=jnp.float32)
    rhs = jnp.concatenate([v * beta[..., None], kb * jnp.exp(gc)[..., None]], axis=-1)
    sol = lax.linalg.triangular_solve(t_mat, rhs, left_side=True, lower=True, unit_diagonal=True)
    u, w = jnp.split(sol, [dv], axis=-1)
    qk = jnp.einsum('bchid,bchjd->bchij', q, k) * decay
    q_dec = q * jnp.exp(gc)[..., None]
    k_dec = k * jnp.exp(gc[..., -1:] - gc)[..., None]
    last = jnp.exp(gc[..., -1])

    def step(state, inp):
        u_c, w_c, qk_c, qd_c, kd_c, last_c = inp
        v_new = u_c - jnp.einsum('bhld,bhdv->bhlv', w_c, state)
        o = jnp.einsum('bhld,bhdv->bhlv', qd_c, state) + jnp.einsum('bhij,bhjv->bhiv', qk_c, v_new)
        state = state * last_c[..., None, None] + jnp.einsum('bhld,bhlv->bhdv', kd_c, v_new)
        return state, o

    xs = tuple(jnp.moveaxis(t, 1, 0) for t in (u, w, qk, q_dec, k_dec, last))
    _, o = lax.scan(step, jnp.zeros((bsz, h, dk, dv), jnp.float32), xs)
    return jnp.transpose(o, (1, 0, 3, 2, 4)).reshape(bsz, s, h, dv)

def gdn_branch(qkv, gate, b_raw, a_raw, conv_w, dt_bias, a_log, norm_g):
    dtype = qkv.dtype
    f32 = jnp.float32
    qkv = jax.nn.silu(causal_dwconv(qkv, conv_w)).astype(f32)
    q, k, v = jnp.split(qkv, [GDN_KEY, 2 * GDN_KEY], axis=-1)
    bsz, s, _ = q.shape
    q = l2_normalize(q.reshape(bsz, s, GDN_HEADS, GDN_DK))
    k = l2_normalize(k.reshape(bsz, s, GDN_HEADS, GDN_DK))
    v = v.reshape(bsz, s, GDN_HEADS, GDN_DV)
    beta = jax.nn.sigmoid(b_raw.astype(f32))
    g = -jnp.exp(a_log.astype(f32)) * jax.nn.softplus(a_raw.astype(f32) + dt_bias.astype(f32))
    o = gated_delta_chunked(q, k, v, g, beta)
    o = o * lax.rsqrt(jnp.mean(o * o, axis=-1, keepdims=True) + EPS) * norm_g.astype(f32)
    o = o.reshape(bsz, s, GDN_VAL) * jax.nn.silu(gate.astype(f32))
    return o.astype(dtype)

def setup_inputs(seed: int = 0) -> dict:
    key = jax.random.key(seed)
    ks = iter(jax.random.split(key, 48))
    f32 = jnp.float32

    def nrm(shape, scale):
        return jax.random.normal(next(ks), shape, f32) * scale

    def gain(n):
        return 1.0 + nrm((DEPTH, n), 0.02)

    def dt_bias(n):
        u = jax.random.uniform(next(ks), (DEPTH, n), f32)
        dt = jnp.exp(u * (math.log(0.1) - math.log(1e-3)) + math.log(1e-3))
        return dt + jnp.log(-jnp.expm1(-dt))

    def a_log(n):
        return jnp.log(jax.random.uniform(next(ks), (DEPTH, n), f32, 1.0, 16.0))

    return {
        'x': nrm((BATCH, SEQ, D_MODEL), 1.0),
        'p': nrm((DEPTH, BATCH, SEQ, PLE_DIM), 1.0),
        'g_mix_pre': gain(D_MODEL),
        'w_in': nrm((DEPTH, D_MODEL, D_IN), D_MODEL ** -0.5),
        'conv_ssm_w': nrm((DEPTH, SSM_CONV, SSM_XBC), SSM_CONV ** -0.5),
        'conv_ssm_b': nrm((DEPTH, SSM_XBC), 0.02),
        'ssm_dt_bias': dt_bias(SSM_HEADS),
        'ssm_a_log': a_log(SSM_HEADS),
        'ssm_d': 1.0 + nrm((DEPTH, SSM_HEADS), 0.02),
        'ssm_norm_g': gain(SSM_D_INNER),
        'conv_gdn_w': nrm((DEPTH, GDN_CONV, GDN_QKV), GDN_CONV ** -0.5),
        'gdn_dt_bias': dt_bias(GDN_HEADS),
        'gdn_a_log': a_log(GDN_HEADS),
        'gdn_norm_g': gain(GDN_DV),
        'w_br_ssm': nrm((DEPTH, SSM_D_INNER, D_MODEL), SSM_D_INNER ** -0.5),
        'w_br_gdn': nrm((DEPTH, GDN_VAL, D_MODEL), GDN_VAL ** -0.5),
        'w_out': nrm((DEPTH, D_MODEL, D_MODEL), D_MODEL ** -0.5),
        'g_mix_post': gain(D_MODEL),
        'g_ffn_pre': gain(D_MODEL),
        'w_ffn_gate': nrm((DEPTH, D_MODEL, D_FF), D_MODEL ** -0.5),
        'w_ffn_up': nrm((DEPTH, D_MODEL, D_FF), D_MODEL ** -0.5),
        'conv_ffn_w': nrm((DEPTH, FFN_CONV, D_FF), FFN_CONV ** -0.5),
        'conv_ffn_b': nrm((DEPTH, D_FF), 0.02),
        'w_ffn_down': nrm((DEPTH, D_FF, D_MODEL), D_FF ** -0.5),
        'g_ffn_post': gain(D_MODEL),
        'w_ple_gate': nrm((DEPTH, D_MODEL, D_MODEL), D_MODEL ** -0.5),
        'w_ple_proj': nrm((DEPTH, PLE_DIM, D_MODEL), PLE_DIM ** -0.5),
        'g_ple_post': gain(D_MODEL),
    }

def reference(x, p, g_mix_pre, w_in, conv_ssm_w, conv_ssm_b, ssm_dt_bias, ssm_a_log, ssm_d, ssm_norm_g,
              conv_gdn_w, gdn_dt_bias, gdn_a_log, gdn_norm_g, w_br_ssm, w_br_gdn, w_out, g_mix_post,
              g_ffn_pre, w_ffn_gate, w_ffn_up, conv_ffn_w, conv_ffn_b, w_ffn_down, g_ffn_post,
              w_ple_gate, w_ple_proj, g_ple_post):
    for i in range(DEPTH):
        h = rms_norm(x, g_mix_pre[i])
        proj = h @ w_in[i]
        z, xbc, dt_raw, qkv, gate, b_raw, a_raw, m_gate = jnp.split(proj, IN_SPLITS, axis=-1)
        y_ssm = mamba2_branch(z, xbc, dt_raw, conv_ssm_w[i], conv_ssm_b[i], ssm_dt_bias[i],
                              ssm_a_log[i], ssm_d[i], ssm_norm_g[i])
        y_gdn = gdn_branch(qkv, gate, b_raw, a_raw, conv_gdn_w[i], gdn_dt_bias[i], gdn_a_log[i],
                           gdn_norm_g[i])
        gate_ssm, gate_gdn = jnp.split(jax.nn.sigmoid(m_gate), 2, axis=-1)
        mixed = gate_ssm * (y_ssm @ w_br_ssm[i]) + gate_gdn * (y_gdn @ w_br_gdn[i])
        x = x + rms_norm(mixed @ w_out[i], g_mix_post[i])
        h = rms_norm(x, g_ffn_pre[i])
        act = jax.nn.gelu(causal_dwconv(h @ w_ffn_gate[i], conv_ffn_w[i]) + conv_ffn_b[i], approximate=True)
        f = (act * (h @ w_ffn_up[i])) @ w_ffn_down[i]
        x = x + rms_norm(f, g_ffn_post[i])
        e = jax.nn.sigmoid(x @ w_ple_gate[i]) * (p[i].astype(x.dtype) @ w_ple_proj[i])
        x = x + rms_norm(e, g_ple_post[i])
    return x


_drawn_inputs = setup_inputs


def setup_inputs(seed=0):
    import zlib

    import numpy as np

    out = dict(_drawn_inputs(seed))
    spreads = {}
    factors = {'conv_ssm_b': 2.932,
     'ssm_d': 30.17,
     'ssm_norm_g': 14.146,
     'gdn_norm_g': 23.2,
     'g_mix_post': 3.819,
     'g_ffn_pre': 3.847,
     'conv_ffn_b': 5.469,
     'g_ffn_post': 19.242,
     'g_ple_post': 28.633}
    for name, (base, spread) in spreads.items():
        noise = np.random.default_rng([zlib.crc32(name.encode()), seed]).standard_normal(out[name].shape)
        drawn = base * np.exp(spread * noise) if base else spread * noise
        out[name] = __import__('jax').numpy.asarray(drawn.astype(out[name].dtype))
    for name, factor in factors.items():
        out[name] = (out[name] * factor).astype(out[name].dtype)
    return out
```

```python
import numpy as np
import concourse.bass as bass
from concourse import mybir
from concourse.alu_op_type import AluOpType as ALU
from contextlib import ExitStack

D_MODEL, SEQ = 1024, 1024
P = 128
KD = D_MODEL // P
NCH = SEQ // P
SSM_HEADS, SSM_HEAD_DIM, SSM_GROUPS = 16, 64, 2
HPG = SSM_HEADS // SSM_GROUPS
GDN_HEADS, GDN_DK = 8, 128
PLE_DIM = 256
D_FF = 4096
EPS = 1e-6
XBC_T, QKV_T, Z_T, GATE_T, MG_T = 12, 24, 8, 8, 16
COL_Z, COL_XBC, COL_DT = 0, 1024, 2560
COL_QKV = COL_DT + SSM_HEADS
COL_GATE = COL_QKV + 3072
COL_B = COL_GATE + 1024
COL_A = COL_B + GDN_HEADS
COL_MG = COL_A + GDN_HEADS
ROW_DT, ROW_A, ROW_B, ROW_U = 0, 32, 64, 96
J_XS, J_BC, J_Q, J_K, J_V, J_Z, J_GATE, J_MG = 0, 8, 12, 20, 28, 36, 44, 52
N_SPILL = 68
FFN_GROUPS = D_FF // (2 * P)
NBUF = 4
BIG = 1.0e30
TM_DT, TM_CUM, TM_EXP, TM_BETA, TM_WD, TM_LAST, N_TM = range(7)
N_LEVEL = 7                                

def hybrid_block_kernel(nc, x, p, g_mix_pre, w_in, conv_ssm_w, conv_ssm_b, ssm_dt_bias, ssm_a_log, ssm_d, ssm_norm_g,
                        conv_gdn_w, gdn_dt_bias, gdn_a_log, gdn_norm_g, w_br_ssm, w_br_gdn, w_out, g_mix_post,
                        g_ffn_pre, w_ffn_gate, w_ffn_up, conv_ffn_w, conv_ffn_b, w_ffn_down, g_ffn_post,
                        w_ple_gate, w_ple_proj, g_ple_post, out):
    f32, f32r, i32 = mybir.dt.float32, mybir.dt.float32r, mybir.dt.int32
    ACT = mybir.ActivationFunctionType
    ds = bass.ds

    def scratch(name, shape):
        return nc.dram_tensor(name, shape, f32).ap()

    spill = scratch("spill", [N_SPILL, P, SEQ])
    x_cm = scratch("x_cm", [KD, P, SEQ])
    p_cm = scratch("p_cm", [2, P, SEQ])
    x1_cm = scratch("x1_cm", [KD, P, SEQ])
    cum_rows = scratch("cum_rows", [P, SEQ])
    y_cm = scratch("y_cm", [16, P, P + SEQ])

    ctx = ExitStack()
    ctx.__enter__()

    def sb(name, shape, dt=f32, c=None):
        return (c or ctx).enter_context(nc.sbuf_tensor(name, shape, dt))

    def sem(name):
        return ctx.enter_context(nc.semaphore(name))

    w_raw = sb("w_raw", [P, 2, 2048])
    w_hi = sb("w_hi", [P, 2, 1024], f32r)
    w_lo = sb("w_lo", [P, 2, 1024], f32r)
    ident = sb("ident", [P, P])
    ones = sb("ones", [P, P])
    eps_t = sb("eps_t", [P, 1])
    par = sb("par", [P, 4, P])
    d_ch = sb("d_ch", [P, KD])
    PR = {}
    at = 0
    for name, n in (("g_mix_pre", 8), ("g_mix_post", 8), ("g_ffn_pre", 8), ("g_ffn_post", 8), ("g_ple_post", 8),
                    ("ssm_norm_g", 8), ("gdn_norm_g", 1), ("conv_ssm_b", 12), ("conv_ffn_b", 32)):
        PR[name] = at
        at += n
    assert at <= P
    PR["conv_ssm_w"], PR["conv_gdn_w"], PR["conv_ffn_w"] = P, 2 * P, 3 * P
    par_f = par[:, :, :].rearrange("p a b -> p (a b)")

    def pcol(name, i=0):
        return par_f[:, PR[name] + i:PR[name] + i + 1]

    def pcol_at(name, i, it, per):
        return par_f[:, ds(it * per + (PR[name] + i), 1)]

    ps = ctx.enter_context(nc.psum_tensor("ps", [P, 8, 512], f32))

    def buf(b):
        return ps[:, 2 * b:2 * b + 2, :].rearrange("p a n -> p (a n)")

    ph12 = ExitStack()
    tmh = sb("tmh", [P, NCH, N_TM, P], f32, ph12)
    hv = sb("hv", [P, 4], f32, ph12)
    tri = sb("tri", [P, P], f32, ph12)
    m_incl = sb("m_incl", [P, P], f32, ph12)
    m_strict = sb("m_strict", [P, P], f32, ph12)
    ph1 = ExitStack()
    act_hi = sb("act_hi", [P, KD, SEQ], f32r, ph1)
    act_lo = sb("act_lo", [P, KD, SEQ], f32r, ph1)
    ring_a = sb("ring_a", [P, 2, SEQ], f32, ph1)
    ring_b = sb("ring_b", [P, 2, SEQ], f32, ph1)
    sub = ExitStack()
    tile_f = sb("tile_f", [P, KD, SEQ], f32, sub)
    xrow = sb("xrow", [P, 2, SEQ], f32, sub)
    stage = sb("stage", [P, 4, P], f32, sub)
    prow = sb("prow", [P, NCH, PLE_DIM], f32, sub)
    rstd = sb("rstd", [P, SEQ], f32, sub)
    sub.close()
    sub = ExitStack()
    xin = sb("xin", [P, 2, SEQ + 4], f32, sub)
    hrow = sb("hrow", [P, 4, SEQ], f32, sub)
    sub.close()
    ph1.close()
    ph2 = ExitStack()
    xbc = sb("xbc", [P, XBC_T, P], f32, ph2)
    qkv = sb("qkv", [P, QKV_T, P], f32, ph2)
    zt = sb("zt", [P, KD, P], f32, ph2)
    gt = sb("gt", [P, KD, P], f32, ph2)
    dec = sb("dec", [P, 32, P], f32, ph2)
    qkn = sb("qkn", [P, 16, P], f32, ph2)
    sqn = sb("sqn", [P, 16, P], f32, ph2)
    cs = sb("cs", [P, N_TM, P], f32, ph2)
    xc = sb("xc", [P, SSM_HEADS, SSM_HEAD_DIM], f32, ph2)
    xcd = sb("xcd", [P, SSM_HEADS, SSM_HEAD_DIM], f32, ph2)
    b_tm = sb("b_tm", [P, SSM_GROUPS, P], f32, ph2)
    bv = sb("bv", [P, GDN_HEADS, P], f32, ph2)
    kdec = sb("kdec", [P, GDN_HEADS, P], f32, ph2)
    inv = sb("inv", [P, GDN_HEADS, P], f32, ph2)
    inv_t = sb("inv_t", [P, GDN_HEADS, P], f32, ph2)
    prod = sb("prod", [P, GDN_HEADS, P], f32, ph2)
    rhs = sb("rhs", [P, GDN_HEADS, P], f32, ph2)
    vnew = sb("vnew", [P, GDN_HEADS, P], f32, ph2)
    qs = sb("qs", [P, GDN_HEADS, P], f32, ph2)
    osq = sb("osq", [P, GDN_HEADS, P], f32, ph2)
    orst = sb("orst", [P, GDN_HEADS], f32, ph2)
    s_ssm = sb("s_ssm", [P, SSM_HEADS, SSM_HEAD_DIM], f32, ph2)
    s_gdn = sb("s_gdn", [P, GDN_HEADS, P], f32, ph2)
    ysum = sb("ysum", [P, D_MODEL], f32, ph2)
    xd = sb("xd", [P, KD, P], f32, ph2)
    yssm = sb("yssm", [P, KD, P], f32, ph2)
    ysq = sb("ysq", [P, KD, P], f32, ph2)
    yrs = sb("yrs", [P, SSM_GROUPS, P], f32, ph2)
    ygdn = sb("ygdn", [P, KD, P], f32, ph2)
    lmask = sb("lmask", [P, N_LEVEL, P], i32, ph2)
    lmask_t = sb("lmask_t", [P, N_LEVEL, P], i32, ph2)
    ph2.close()
    ph12.close()
    ph3 = ExitStack()
    act_hi3 = sb("act_hi3", [P, KD, SEQ], f32r, ph3)
    act_lo3 = sb("act_lo3", [P, KD, SEQ], f32r, ph3)
    tile3 = sb("tile3", [P, KD, SEQ], f32, ph3)
    ring3 = sb("ring3", [P, 2, SEQ], f32, ph3)
    sub = ExitStack()
    mg3 = sb("mg3", [P, 2, SEQ], f32, sub)
    sq3 = sb("sq3", [P, 2, SEQ], f32, sub)
    res3 = sb("res3", [P, 2, SEQ], f32, sub)
    rs3 = sb("rs3", [P, SEQ], f32, sub)
    acc3 = sb("acc3", [P, SEQ], f32, sub)
    sub.close()
    sub = ExitStack()
    f_hi = sb("f_hi", [P, 2, 2, SEQ], f32r, sub)
    f_lo = sb("f_lo", [P, 2, 2, SEQ], f32r, sub)
    fa = sb("fa", [P, 2, SEQ], f32, sub)
    xin3 = sb("xin3", [P, SEQ + 4], f32, sub)
    sub.close()
    sub = ExitStack()
    pj = sb("pj", [P, KD, SEQ], f32, sub)
    fa_again = sb("fa_again", [P, 2, SEQ], f32, sub)
    p_hi4 = sb("p_hi4", [P, 2, SEQ], f32r, sub)
    p_lo4 = sb("p_lo4", [P, 2, SEQ], f32r, sub)
    res4 = sb("res4", [P, 2, SEQ], f32, sub)
    sub.close()
    ph3.close()

    x_rows = x.rearrange("o (t q) d -> (o t) q d", q=P)
    p_rows = p.rearrange("l o (t q) d -> q (l o t) d", q=P)
    out_rows = out.rearrange("o (t q) d -> (o t) q d", q=P)
    w_in_k = w_in.rearrange("l (k q) n -> q (l k) n", q=P)
    spill_c = spill.rearrange("j q t -> q j t")

    def weights_k(w):
        return w.rearrange("l (k q) n -> q (l k) n", q=P)

    consts_done = sem("consts_done")
    params_in = sem("params_in")
    hv_in = sem("hv_in")
    hv_done = sem("hv_done")
    x_in = [sem(f"x_in{i}") for i in range(2)]
    p_in = sem("p_in")
    xt_kept = sem("xt_kept")
    pt_kept = sem("pt_kept")
    small_in = sem("small_in")
    raw_in = [sem(f"raw_in{i}") for i in range(2)]
    unit_begun = sem("unit_begun")
    pool_met, dve_met = sem("pool_met"), sem("dve_met")
    split_done = sem("split_done")
    tile_done = [sem(f"tile_done{i}") for i in range(NBUF)]
    tile_free = [sem(f"tile_free{i}") for i in range(NBUF)]
    norm_sq = sem("norm_sq")
    norm_sum = sem("norm_sum")
    pads_done = sem("pads_done")
    norm_rs = sem("norm_rs")
    norm_h = sem("norm_h")
    hi_done = sem("hi_done")
    lo_done = sem("lo_done")
    head_act = sem("head_act")
    head_dve = sem("head_dve")
    tm_dve = sem("tm_dve")
    tm_act = sem("tm_act")
    cum_kept = sem("cum_kept")
    conv_step = sem("conv_step")
    conv_out = sem("conv_out")
    spilled = [sem(f"spilled{i}") for i in range(2)]

    in_xbc, in_qkv, in_z, in_g = (sem(n) for n in ("in_xbc", "in_qkv", "in_z", "in_g"))
    in_dec_s, in_dec_n, in_dec_q = (sem(n) for n in ("in_dec_s", "in_dec_n", "in_dec_q"))
    out_zero = sem("out_zero")
    ys_kept, yg_kept = sem("ys_kept"), sem("yg_kept")
    seg_done = sem("seg_done")
    state_zero, iota_done, xd_ready, xcd_ready, inv_init, s_ssm_dec, s_gdn_dec = (
        sem(n) for n in ("state_zero", "iota_done", "xd_ready", "xcd_ready", "inv_init", "s_ssm_dec", "s_gdn_dec"))
    xt_done, bt_done, vt_done, kt_done, nt_done, yt_done, ot_done = (
        sem(n) for n in ("xt_done", "bt_done", "vt_done", "kt_done", "nt_done", "yt_done", "ot_done"))
    sc_done, qk_sum, gram_mm, diag_done, off_done, st_done, yssq_done = (
        sem(n) for n in ("sc_done", "qk_sum", "gram_mm", "diag_done", "off_done", "st_done", "yssq_done"))
    prod_done, upd_mm, ks_done, qs_done, vn_done, o_done, ds_done = (
        sem(n) for n in ("prod_done", "upd_mm", "ks_done", "qs_done", "vn_done", "o_done", "ds_done"))
    qk_sq, qk_rs, dec_exp, b_copied, prod_copied, vn_copied, ysq_done, yrs_done, osq_done, orst_done = (
        sem(n) for n in ("qk_sq", "qk_rs", "dec_exp", "b_copied", "prod_copied", "vn_copied", "ysq_done", "yrs_done",
                         "osq_done", "orst_done"))
    cs_ready, x_scaled, v_scaled, qk_normed, k_scaled, m_ready, gram_done = (
        sem(n) for n in ("cs_ready", "x_scaled", "v_scaled", "qk_normed", "k_scaled", "m_ready", "gram_done"))
    mask_step, y_sum, s_ssm_new, y_mid, y_out, inv_step = (
        sem(n) for n in ("mask_step", "y_sum", "s_ssm_new", "y_mid", "y_out", "inv_step"))
    r_step, qs_scaled, s_gdn_new, o_sum, o_ssq, o_normed, yg_out = (
        sem(n) for n in ("r_step", "qs_scaled", "s_gdn_new", "o_sum", "o_ssq", "o_normed", "yg_out"))
    y_c = y_cm.rearrange("j q t -> q j t")
    N_CONST, N_PARAM_DMA = 15, 14

    def branch_weights(which, n):
        return weights_k((w_br_ssm, w_br_gdn)[which])[:, :, n * 256:(n + 1) * 256]

    y_in, mg_in, res_in, res4_in, out_kept = (
        [sem(f"{n}{i}") for i in range(2)] for n in ("y_in", "mg_in", "res_in", "res4_in", "out_kept"))
    p4_in, x1_kept = sem("p4_in"), sem("x1_kept")
    gated, mixed, acc_done, x1_step, x2_step, e_done, fin_step = (
        sem(n) for n in ("gated", "mixed", "acc_done", "x1_step", "x2_step", "e_done", "fin_step"))
    sq_done, gelu_done, f_hi_done, p_hi_done, fconv, f_lo_done, p_lo_done = (
        sem(n) for n in ("sq_done", "gelu_done", "f_hi_done", "p_hi_done", "fconv", "f_lo_done", "p_lo_done"))

    block = ctx.enter_context(nc.Block())

    U_SMALL, U_PROJ = 0, 1
    O_PAR, O_X, O_P, O_NORM0, O_SMALL = 0, 1, 9, 11, 12
    O_XBC = 13
    O_QKV = O_XBC + XBC_T
    O_TM = O_QKV + QKV_T
    O_Z = O_TM + 2
    O_CUM = O_Z + Z_T
    O_GATE = O_CUM + 3
    O_MG = O_GATE + GATE_T
    O_BRS = O_MG + MG_T
    U_BRS = 1 + N_SPILL
    PROJ = [("ssm", COL_XBC, 4, J_XS, O_XBC), ("ssm", COL_XBC + 4 * P, XBC_T - 4, J_XS + 4, O_XBC + 4),
            ("gdn", COL_QKV, QKV_T, J_Q, O_QKV), ("silu", COL_Z, Z_T, J_Z, O_Z),
            ("silu", COL_GATE, GATE_T, J_GATE, O_GATE), ("sigmoid", COL_MG, MG_T, J_MG, O_MG)]

    def run_tiles(eng, tiles, j0, body):
        if j0 == 0:
            for n in range(tiles):
                body(None, n)
        else:
            with eng.Fori(0, tiles // 4) as it:
                for n in range(4):
                    body(it, n)

    def uses(o0, n, it=None, per=0):
        c = (o0 + n) // NBUF
        return (o0 + n) % NBUF, c if it is None else it * (per // NBUF) + c

    def wait_tile(eng, o0, n=0, it=None, per=0):
        b, c = uses(o0, n, it, per)
        eng.wait_ge(tile_done[b], c + 1)
        return b

    def wait_buffer(eng, o0, n=0, it=None, per=0):
        b, c = uses(o0, n, it, per)
        if it is not None or c > 0:
            eng.wait_ge(tile_free[b], c)
        return b

    def raw_count(q0, n, it=None, per=0):
        q = q0 + n
        c = 16 * (q // 2 + q % 2)
        return q % 2, c if it is None else it * (8 * per) + c

    def waits_met(eng, sem):
        eng.sem_inc(sem, 1)

    def load_block(eng, src, q0, n, it=None, per=0):
        slot, _ = raw_count(q0, n, it, per)
        if it is None:
            if q0 + n >= 2:
                eng.wait_ge(split_done, 4 * (q0 + n) - 6)
        else:
            eng.wait_ge(split_done, it * (4 * per) + (4 * (q0 + n) - 6))
        eng.dma_start(w_raw[:, slot, :].rearrange("p (k n) -> p k n", k=src.shape[1]), src).then_inc(raw_in[slot], 16)

    def split_unit(pool, u0, n, it=None, per=0, k=KD):
        u = u0 + n
        q = (u + 1) // 2
        slot, half = u % 2, (u + 1) % 2
        if u == 0:
            pool.wait_ge(small_in, 64)
            half = 0
        else:
            count = 16 * (q // 2 + q % 2)
            pool.wait_ge(raw_in[q % 2], count if it is None else it * (4 * per) + count)
        w = 2048 // k
        raw = w_raw[:, q % 2, :].rearrange("p (k n) -> p k n", k=k)[:, :, half * (w // 2):(half + 1) * (w // 2)]
        hi = w_hi[:, slot, :].rearrange("p (k n) -> p k n", k=k)
        lo = w_lo[:, slot, :].rearrange("p (k n) -> p k n", k=k)
        if it is None:
            if u >= 2:
                pool.wait_ge(unit_begun, u)
        else:
            pool.wait_ge(unit_begun, it * per + u)
        waits_met(pool, pool_met)
        nc.gpsimd.tensor_scalar(hi, raw, 1.0, 0.0, ALU.mult, ALU.add).then_inc(split_done, 1)
        pool.wait_ge(split_done, 2 * u + 1 if it is None else it * (2 * per) + (2 * u + 1))
        nc.gpsimd.tensor_tensor(lo, raw, hi.bitcast(f32), ALU.subtract).then_inc(split_done, 1)

    def pe_unit(pe, u0, o0, n, it=None, per=0, mov=None, ready=None, per_o=None):
        mov_hi, mov_lo = mov
        u = u0 + n
        slot = u % 2
        b = wait_buffer(pe, o0, n, it, per_o or per)
        pe.wait_ge(split_done, 2 * u + 2 if it is None else it * (2 * per) + (2 * u + 2))
        for k in range(KD):
            if ready:
                pe.wait_ge(ready[0], ready[1] + k + 1)
            wh, wl = (w[:, slot, k * P:(k + 1) * P] for w in (w_hi, w_lo))
            for half in range(2):
                o = ps[:, 2 * b + half, :]
                c = slice(half * 512, half * 512 + 512)
                first = nc.tensor.matmul(o, wh, mov_hi[:, k, c], start=(k == 0), stop=False)
                if k == 0 and half == 0:
                    first.then_inc(unit_begun, 1)
                nc.tensor.matmul(o, wh, mov_lo[:, k, c], start=False, stop=False)
                last = nc.tensor.matmul(o, wl, mov_hi[:, k, c], start=False, stop=(k == KD - 1))
        last.then_inc(tile_done[b], 1)
        return b



    def pe_norm(pe, o, ring, nth):
        b = wait_buffer(pe, o)
        for k in range(KD):
            pe.wait_ge(norm_sq, KD * nth + k + 1)
            for half in range(2):
                last = nc.tensor.matmul(ps[:, 2 * b + half, :], ones[:, :], ring[:, k % 2, half * 512:half * 512 + 512],
                                        start=(k == 0), stop=(k == KD - 1))
            last.then_inc(norm_sum if k < KD - 1 else tile_done[b], 1)

    def act_norm_factor(act, o, rs, nth):
        b = wait_tile(act, o)
        nc.scalar.activation(rs[:, :], buf(b), ACT.Ln, scale=1.0 / D_MODEL, bias=eps_t[:, 0:1]).then_inc(tile_free[b], 1)
        act.wait_ge(tile_free[b], uses(o, 0)[1] + 1)
        nc.scalar.activation(rs[:, :], rs[:, :], ACT.Exp, scale=-0.5).then_inc(norm_rs, 1)

    def act_norm(act, o, src, ring, rs, nth, ready=None):
        for k in range(KD):
            if k >= 2:
                act.wait_ge(norm_sum, (KD - 1) * nth + k - 1)
            if ready:
                act.wait_ge(ready[0], ready[1] + k + 1)
            nc.scalar.activation(ring[:, k % 2, :], src[:, k, :], ACT.Square).then_inc(norm_sq, 1)
        act_norm_factor(act, o, rs, nth)

    def dve_scale_split(dve, gname, src, ring, rs, hi, lo, nth, base):
        def low(k):
            dve.wait_ge(hi_done, base + k + 1)
            nc.vector.tensor_tensor(lo[:, k, :], ring[:, k % 2, :], hi[:, k, :].bitcast(f32), ALU.subtract).then_inc(lo_done, 1)
        dve.wait_ge(norm_rs, nth + 1)
        for k in range(KD):
            if k >= 2:
                dve.wait_ge(lo_done, base + k - 1)
            nc.vector.scalar_tensor_tensor(out=ring[:, k % 2, :], in0=src[:, k, :], scalar=pcol(gname, k), in1=rs[:, :],
                                           op0=ALU.mult, op1=ALU.mult).then_inc(norm_h, 1)
            if k >= 1:
                low(k - 1)
        low(KD - 1)

    HEAD_SP, HEAD_L, TM_SRC, TM_END = 14, 15, 2, 3

    def head_softplus(dve):
        v, step = nc.vector, [0]
        r = [hrow[:, i, :] for i in range(4)]

        def then(ins):
            ins.then_inc(head_dve, 1)
            step[0] += 1
            dve.wait_ge(head_dve, step[0])

        dve.wait_ge(head_act, 2)
        then(v.tensor_scalar(r[2], r[1], 2.0, None, ALU.add))
        then(v.reciprocal(r[2], r[2]))
        then(v.tensor_tensor(r[2], r[1], r[2], ALU.mult))
        then(v.tensor_tensor(r[3], r[2], r[2], ALU.mult))
        then(v.tensor_scalar(r[1], r[3], 1.0 / 15, None, ALU.mult))
        for odd in (13, 11, 9, 7, 5, 3):
            then(v.scalar_tensor_tensor(out=r[1], in0=r[1], scalar=1.0 / odd, in1=r[3], op0=ALU.add, op1=ALU.mult))
        then(v.scalar_tensor_tensor(out=r[1], in0=r[1], scalar=1.0, in1=r[2], op0=ALU.add, op1=ALU.mult))
        then(v.tensor_scalar(r[0], r[0], 0.0, None, ALU.max))
        then(v.scalar_tensor_tensor(out=r[1], in0=r[1], scalar=2.0, in1=r[0], op0=ALU.mult, op1=ALU.add))
        assert step[0] == HEAD_SP
        dve.wait_ge(hv_done, 2)
        then(v.tensor_scalar(r[2], r[1], hv[:, 3:4], None, ALU.mult))
        assert step[0] == HEAD_L

    def by_chunk(ap):
        return ap.rearrange("p (c r) -> p c r", c=NCH)

    def tm_sources(dve):
        v = nc.vector
        b = wait_tile(dve, O_TM, 0)
        v.tensor_copy(tmh[:, :, TM_DT, :], by_chunk(buf(b))).then_inc(tile_free[b], 1)
        b = wait_tile(dve, O_TM, 1)
        v.tensor_copy(hrow[:, 0, :], buf(b)).then_inc(tile_free[b], 1)
        v.memset(hrow[:, 3, :], 0.0).then_inc(tm_dve, 1)
        dve.wait_ge(tile_free[b], uses(O_TM, 1)[1] + 1)
        dve.wait_ge(tm_dve, 1)
        v.tensor_copy(by_chunk(hrow[:, 3, :])[:, :, ROW_U:ROW_U + GDN_HEADS],
                      by_chunk(hrow[:, 0, :])[:, :, ROW_B:ROW_B + GDN_HEADS]).then_inc(tm_dve, 1)

    def tm_sums(dve):
        v = nc.vector
        b = wait_tile(dve, O_CUM, 0)
        v.tensor_copy(tmh[:, :, TM_CUM, :], by_chunk(buf(b))).then_inc(tile_free[b], 1)
        b = wait_tile(dve, O_CUM, 1)
        v.tensor_copy(hrow[:, 1, :], buf(b)).then_inc(tile_free[b], 1)
        b = wait_tile(dve, O_CUM, 2)
        v.tensor_copy(hrow[:, 2, :], buf(b)).then_inc(tile_free[b], 1)
        for i in (0, 2):
            b, c = uses(O_CUM, i)
            dve.wait_ge(tile_free[b], c + 1)
        v.tensor_tensor(tmh[:, :, TM_WD, :], by_chunk(hrow[:, 2, :]), tmh[:, :, TM_CUM, :], ALU.subtract).then_inc(tm_dve, 1)

    HA = GDN_HEADS // 2
    N_INV = 4 * (N_LEVEL - 1) + 2
    N_UPD = 4 * (N_LEVEL - 2) + 2
    N_PROD = 2 * (N_LEVEL - 1)

    def bank(i, n=1):
        return ps[:, i:i + n, :].rearrange("p a n -> p (a n)")

    def heads_of(batch):
        return slice(batch * HA, batch * HA + HA)

    def wide(ap, n):
        return ap.unsqueeze(2).broadcast_to([P, ap.shape[1], n])

    GIVEN = {
        "sp": (in_xbc, in_qkv, in_z, in_dec_s, in_dec_n, in_dec_q),
        "pool": (seg_done, xd_ready, xcd_ready, inv_init, s_ssm_dec, s_gdn_dec),
        "pe": (xt_done, bt_done, sc_done, qk_sum, vt_done, kt_done, gram_mm, diag_done, off_done, nt_done, st_done, prod_done,
               upd_mm, yt_done, yssq_done, ks_done, qs_done, vn_done, ds_done, o_done, ot_done),
        "act": (in_g, qk_sq, b_copied, qk_rs, dec_exp, prod_copied, ysq_done, yrs_done, vn_copied, osq_done, orst_done, ys_kept, yg_kept),
        "dve": (cs_ready, x_scaled, v_scaled, qk_normed, k_scaled, m_ready, gram_done, y_sum, inv_step, s_ssm_new,
                y_mid, y_out, r_step, qs_scaled, s_gdn_new, o_sum, o_ssq, o_normed, yg_out),
    }

    def give(eng, name):
        for s in GIVEN[name]:
            eng.sem_inc(s, 1)

    def after(eng, s, count):
        eng.wait_ge(s, count + 1)

    def ready_to_mix(eng):
        for i in range(2):
            eng.wait_ge(spilled[i], 16 * (N_SPILL // 2))
        eng.wait_ge(cum_kept, 16)
        eng.wait_ge(tm_act, 4)

    def sp_mixer(sp):
        for n in range(2):
            load_block(sp, branch_weights(0, n), 1 + N_SPILL // 2, n)
        ready_to_mix(sp)
        give(sp, "sp")
        with sp.Fori(0, NCH) as c:
            tok = ds(c * P, P)
            after(sp, off_done, c)
            after(sp, xd_ready, c)
            sp.dma_start(xbc[:, :, :], spill_c[:, 0:XBC_T, tok]).then_inc(in_xbc, 16)
            after(sp, qk_normed, c * 2)
            after(sp, vt_done, c)
            sp.dma_start(qkv[:, :, :], spill_c[:, J_Q:J_Q + QKV_T, tok]).then_inc(in_qkv, 16)
            after(sp, y_mid, c * 2)
            sp.dma_start(zt[:, :, :], spill_c[:, J_Z:J_Z + Z_T, tok]).then_inc(in_z, 16)
            def load_sums(s, row, n, at):
                sp.dma_start(dec[:, at:at + n, :], cum_rows[row:row + n, tok].unsqueeze(0).broadcast_to([P, n, P])).then_inc(s, 16)
            after(sp, diag_done, c * 2)
            load_sums(in_dec_s, ROW_DT, SSM_HEADS, 0)
            after(sp, prod_done, c * N_PROD)
            load_sums(in_dec_n, ROW_U, GDN_HEADS, 24)
            after(sp, o_done, c * 2)
            load_sums(in_dec_q, ROW_A, GDN_HEADS, 16)

    def pool_mixer(pool):
        g = nc.gpsimd
        split_unit(pool, U_BRS, 0)
        ready_to_mix(pool)
        g.memset(s_ssm[:, :, :], 0.0).then_inc(state_zero, 1)
        g.memset(s_gdn[:, :, :], 0.0).then_inc(state_zero, 1)
        osi = osq[:, :, :].bitcast(i32)
        g.iota(osi[:, 0, :], [[0, P]], base=0, channel_multiplier=1).then_inc(iota_done, 1)
        g.iota(osi[:, 1, :], [[1, P]], base=0, channel_multiplier=0).then_inc(iota_done, 1)
        pool.wait_ge(state_zero, 2)
        give(pool, "pool")
        with pool.Fori(0, NCH) as c:
            def log_decays(nth, loaded, at, n, row, mask):
                d = dec[:, at:at + n, :]
                sums = tmh[:, ds(c, 1), TM_CUM, row:row + n].rearrange("p o r -> p (o r)")
                after(pool, loaded, c * 16 + 16)
                waits_met(pool, pool_met)
                g.tensor_tensor(d, d, wide(sums, P), ALU.subtract).then_inc(seg_done, 1)
                after(pool, seg_done, c * 6 + (2 * nth + 1))
                g.tensor_tensor(d, d, mask[:, :].unsqueeze(1).broadcast_to([P, n, P]), ALU.add).then_inc(seg_done, 1)

            log_decays(0, in_dec_s, 0, SSM_HEADS, ROW_DT, m_incl)
            log_decays(1, in_dec_n, 24, GDN_HEADS, ROW_A, m_strict)
            log_decays(2, in_dec_q, 16, GDN_HEADS, ROW_A, m_incl)
            ident_wide = ident[:, :].unsqueeze(1).broadcast_to([P, GDN_HEADS, P])
            after(pool, vn_done, c * 2)
            waits_met(pool, pool_met)
            for m in (inv, inv_t):
                g.tensor_tensor(m[:, :, :], ident_wide, ones[:, :].unsqueeze(1).broadcast_to([P, GDN_HEADS, P]),
                                ALU.mult).then_inc(inv_init, 1)
            after(pool, cs_ready, c + 1)
            after(pool, x_scaled, c + 1)
            after(pool, st_done, c)
            g.tensor_tensor(xcd[:, :, :], xc[:, :, :], wide(cs[:, TM_WD, ROW_DT:ROW_DT + SSM_HEADS], SSM_HEAD_DIM),
                            ALU.mult).then_inc(xcd_ready, 1)
            after(pool, in_xbc, c * 16 + 16)
            after(pool, y_mid, c * 2)
            g.tensor_tensor(xd[:, :, :], xbc[:, 0:KD, :], wide(d_ch[:, :], P), ALU.mult).then_inc(xd_ready, 1)
            after(pool, off_done, c + 1)
            g.tensor_tensor(s_ssm[:, :, :], s_ssm[:, :, :],
                            wide(cs[:, TM_LAST, ROW_DT:ROW_DT + SSM_HEADS], SSM_HEAD_DIM), ALU.mult).then_inc(s_ssm_dec, 1)
            for batch in range(2):
                after(pool, qs_done, c * 2 + (batch + 1))
                h = heads_of(batch)
                g.tensor_tensor(s_gdn[:, h, :], s_gdn[:, h, :],
                                wide(cs[:, TM_LAST, ROW_A + h.start:ROW_A + h.stop], P), ALU.mult).then_inc(s_gdn_dec, 1)

    def pe_mixer(pe):
        t = nc.tensor
        ready_to_mix(pe)
        pe.wait_ge(state_zero, 2)
        for b in range(NBUF):
            pe.wait_ge(tile_free[b], (O_BRS - 1 - b) // NBUF + 1)
        give(pe, "pe")

        def gdn_out(n):
            after(pe, o_normed, n + 1)
            for h in range(GDN_HEADS):
                last = t.transpose(bank(6, 2)[:, h * P:(h + 1) * P], qs[:, h, :], ident[:, :])
            last.then_inc(ot_done, 1)

        with pe.Fori(0, NCH) as c:
            after(pe, in_xbc, c * 16 + 16)
            after(pe, vn_copied, c * 2)
            for k in range(KD):
                last = t.transpose(bank(4, 2)[:, k * P:(k + 1) * P], xbc[:, k, :], ident[:, :])
            last.then_inc(xt_done, 1)
            for i, at in enumerate((8, 0)):
                if i == 0:
                    after(pe, qs_scaled, c * 2)
                else:
                    after(pe, s_gdn_new, c * 2)
                after(pe, qk_sq, c * 2 + (i + 1))
                for half in range(2):
                    last = t.matmul(bank(2 - 2 * i + half), ones[:, :],
                                    sqn[:, at + 4 * half:at + 4 * half + 4, :].rearrange("p h t -> p (h t)"), start=True, stop=True)
                last.then_inc(qk_sum, 1)
            after(pe, o_sum, c * 2)
            for g in range(SSM_GROUPS):
                last = t.transpose(bank(6)[:, g * P:(g + 1) * P], xbc[:, KD + g, :], ident[:, :])
            last.then_inc(bt_done, 1)
            for g in range(SSM_GROUPS):
                last = t.matmul(bank(7)[:, g * P:(g + 1) * P], xbc[:, KD + g, :], xbc[:, KD + 2 + g, :], start=True, stop=True)
            last.then_inc(sc_done, 1)
            after(pe, in_qkv, c * 16 + 16)
            after(pe, x_scaled, c + 1)
            for h in range(GDN_HEADS):
                last = t.transpose(bank(4, 2)[:, h * P:(h + 1) * P], qkv[:, 16 + h, :], ident[:, :])
            last.then_inc(vt_done, 1)
            after(pe, qk_rs, c * 4 + 2)
            after(pe, s_ssm_new, c)
            for g in range(SSM_GROUPS):
                last = t.matmul(bank(g), xbc[:, KD + 2 + g, :],
                                s_ssm[:, g * HPG:(g + 1) * HPG, :].rearrange("p h d -> p (h d)"), start=True, stop=True)
            last.then_inc(off_done, 1)

            def diag(g):
                for i in range(HPG):
                    h = g * HPG + i
                    last = t.matmul(bank(2, 2)[:, i * P:(i + 1) * P], dec[:, h, :],
                                    xc[:, h - h % 2:h - h % 2 + 2, :].rearrange("p h d -> p (h d)"), start=True, stop=True)
                last.then_inc(diag_done, 1)

            after(pe, m_ready, c * 2 + 1)
            diag(0)
            after(pe, qk_normed, c * 2 + 1)
            after(pe, v_scaled, c + 1)
            for h in range(GDN_HEADS):
                last = t.transpose(bank(4, 2)[:, h * P:(h + 1) * P], qkn[:, 8 + h, :], ident[:, :])
            last.then_inc(kt_done, 1)
            after(pe, qk_normed, c * 2 + 2)
            for batch in range(2):
                if batch == 0:
                    after(pe, y_sum, c * 3 + 2)
                else:
                    after(pe, k_scaled, c + 1)
                for h in range(batch * HA, batch * HA + HA):
                    last = t.matmul(bank(2, 4)[:, h * 2 * P:(h + 1) * 2 * P].rearrange("p (a t) -> p a t", a=2),
                                    qkn[:, 8 + h, :], qkn[:, h:h + 9:8, :], start=True, stop=True)
                last.then_inc(gram_mm, 1)
            after(pe, b_copied, c + 1)
            after(pe, m_ready, c * 2 + 2)
            for batch in range(2):
                after(pe, gram_done, c * 4 + (batch + 1))
                for h in range(HA):
                    last = t.transpose(bank(6 + batch)[:, h * P:(h + 1) * P], dec[:, 24 + batch * HA + h, :], ident[:, :])
                last.then_inc(nt_done, 1)
            after(pe, gram_done, c * 4 + 3)
            diag(1)
            for lv in range(1, N_LEVEL):
                for batch in range(2):
                    if lv == 1:
                        after(pe, y_sum, c * 3 + 1)
                    after(pe, inv_step, c * N_INV + (4 * (lv - 1) + 2 * batch + 2))
                    for h in range(HA):
                        hh = batch * HA + h
                        last = t.matmul(bank(batch)[:, h * P:(h + 1) * P], dec[:, 24 + hh, :], inv[:, hh, :], start=True, stop=True)
                    last.then_inc(prod_done, 1)
                if lv == 1:
                    after(pe, xcd_ready, c + 1)
                    after(pe, inv_step, c * N_INV + 4)
                    for g in range(SSM_GROUPS):
                        last = t.matmul(bank(6 + g), b_tm[:, g, :],
                                        xcd[:, g * HPG:(g + 1) * HPG, :].rearrange("p h d -> p (h d)"), start=True, stop=True)
                    last.then_inc(st_done, 1)
                for batch in range(2):
                    after(pe, prod_copied, c * N_PROD + (2 * (lv - 1) + batch + 1))
                    if lv < N_LEVEL - 1:
                        if lv == 1:
                            after(pe, y_sum, c * 3 + 3)
                            after(pe, gram_done, c * 4 + 4)
                        for h in range(HA):
                            hh = batch * HA + h
                            last = t.matmul(bank(2 + batch)[:, h * P:(h + 1) * P], inv_t[:, hh, :], prod[:, hh, :], start=True, stop=True)
                        last.then_inc(upd_mm, 1)
                    for h in range(HA):
                        hh = batch * HA + h
                        last = t.matmul(bank(4 + batch)[:, h * P:(h + 1) * P], prod[:, hh, :], inv_t[:, hh, :], start=True, stop=True)
                    last.then_inc(upd_mm, 1)
                if lv == 1:
                    after(pe, s_ssm_new, c + 1)
                    for k in range(KD):
                        last = t.transpose(bank(6, 2)[:, k * P:(k + 1) * P], ysum[:, k * P:(k + 1) * P], ident[:, :])
                    last.then_inc(yt_done, 1)
                if lv == 3:
                    after(pe, ysq_done, c + 1)
                    for g in range(SSM_GROUPS):
                        for k in range(4):
                            last = t.matmul(bank(6)[:, g * P:(g + 1) * P], ones[:, :], ysq[:, 4 * g + k, :], start=(k == 0), stop=(k == 3))
                    last.then_inc(yssq_done, 1)
                if lv == 5:
                    after(pe, yrs_done, c * 2 + 1)
                    gdn_out(c)
            after(pe, s_gdn_new, c * 2)
            for batch in range(2):
                for h in range(HA):
                    hh = batch * HA + h
                    last = t.matmul(bank(batch)[:, h * P:(h + 1) * P], qkn[:, 8 + hh, :], s_gdn[:, hh, :], start=True, stop=True)
                last.then_inc(ks_done, 1)
            for batch in range(2):
                for h in range(HA):
                    hh = batch * HA + h
                    last = t.matmul(bank(2 + batch)[:, h * P:(h + 1) * P], qkn[:, hh, :], s_gdn[:, hh, :], start=True, stop=True)
                last.then_inc(qs_done, 1)
            for batch in range(2):
                after(pe, inv_step, c * N_INV + (N_INV - 1 + batch))
                after(pe, r_step, c * 4 + (2 * batch + 2))
                for h in range(HA):
                    hh = batch * HA + h
                    last = t.matmul(bank(4 + batch)[:, h * P:(h + 1) * P], inv_t[:, hh, :], rhs[:, hh, :], start=True, stop=True)
                last.then_inc(vn_done, 1)
            after(pe, yg_out, c + 1)
            for batch in range(2):
                after(pe, vn_copied, c * 2 + (batch + 1))
                for h in range(HA):
                    hh = batch * HA + h
                    last = t.matmul(bank(batch)[:, h * P:(h + 1) * P], kdec[:, hh, :], vnew[:, hh, :], start=True, stop=True)
                last.then_inc(ds_done, 1)
                for h in range(HA):
                    hh = batch * HA + h
                    last = t.matmul(bank(6 + batch)[:, h * P:(h + 1) * P], dec[:, 16 + hh, :], vnew[:, hh, :], start=True, stop=True)
                last.then_inc(o_done, 1)
        after(pe, o_sum, 2 * NCH)
        gdn_out(NCH)

    def act_mixer(act):
        a = nc.scalar.activation
        ready_to_mix(act)
        give(act, "act")

        def out_squares(n):
            after(act, o_sum, n * 2)
            after(act, o_ssq, n)
            a(osq[:, :, :], qs[:, :, :], ACT.Square).then_inc(osq_done, 1)

        def out_ln(n):
            after(act, o_ssq, n + 1)
            a(orst[:, :], orst[:, :], ACT.Ln, scale=1.0 / P, bias=eps_t[:, 0:1]).then_inc(orst_done, 1)

        def out_exp(n):
            after(act, orst_done, n * 2 + 1)
            a(orst[:, :], orst[:, :], ACT.Exp, scale=-0.5).then_inc(orst_done, 1)

        def out_store(n):
            after(act, yg_out, n + 1)
            act.dma_start(y_c[:, KD:2 * KD, ds(n * P, P)], ygdn[:, :, :]).then_inc(yg_kept, 16)

        with act.Fori(0, NCH) as c:
            after(act, in_qkv, c * 16 + 16)
            after(act, qk_normed, c * 2)
            for at in (8, 0):
                a(sqn[:, at:at + 8, :], qkv[:, at:at + 8, :], ACT.Square).then_inc(qk_sq, 1)
            after(act, seg_done, c * 6 + 2)
            a(dec[:, 0:16, :], dec[:, 0:16, :], ACT.Exp).then_inc(dec_exp, 1)
            flat = [sqn[:, at:at + 8, :].rearrange("p h t -> p (h t)") for at in (8, 0)]
            for i in range(2):
                after(act, qk_sum, c * 2 + (i + 1))
                a(flat[i], bank(2 - 2 * i, 2), ACT.Ln, bias=eps_t[:, 0:1]).then_inc(qk_rs, 1)
            for i in range(2):
                after(act, qk_rs, c * 4 + (i + 1))
                a(flat[i], flat[i], ACT.Exp, scale=-0.5).then_inc(qk_rs, 1)
            after(act, seg_done, c * 6 + 4)
            a(dec[:, 24:32, :], dec[:, 24:32, :], ACT.Exp).then_inc(dec_exp, 1)
            after(act, bt_done, c + 1)
            after(act, st_done, c)
            a(b_tm[:, :, :].rearrange("p g n -> p (g n)"), bank(6)[:, 0:2 * P], ACT.Copy).then_inc(b_copied, 1)
            after(act, seg_done, c * 6 + 6)
            a(dec[:, 16:24, :], dec[:, 16:24, :], ACT.Exp).then_inc(dec_exp, 1)
            for lv in range(1, N_LEVEL):
                for batch in range(2):
                    after(act, prod_done, c * N_PROD + (2 * (lv - 1) + batch + 1))
                    after(act, upd_mm, c * N_UPD + (4 * (lv - 2) + 2 * batch + 2 if lv > 1 else 0))
                    a(prod[:, heads_of(batch), :].rearrange("p h t -> p (h t)"), bank(batch), ACT.Copy).then_inc(prod_copied, 1)
                if lv == 2:
                    after(act, y_mid, c * 2 + 2)
                    after(act, yssq_done, c)
                    a(ysq[:, :, :], yssm[:, :, :], ACT.Square).then_inc(ysq_done, 1)
                    out_squares(c)
                if lv == 4:
                    after(act, yssq_done, c + 1)
                    after(act, y_out, c)
                    f = yrs[:, :, :].rearrange("p g t -> p (g t)")
                    a(f, bank(6)[:, 0:2 * P], ACT.Ln, scale=1.0 / 512, bias=eps_t[:, 0:1]).then_inc(yrs_done, 1)
                    out_ln(c)
                    after(act, yrs_done, c * 2 + 1)
                    a(f, f, ACT.Exp, scale=-0.5).then_inc(yrs_done, 1)
                    out_exp(c)
            after(act, y_out, c + 1)
            act.dma_start(y_c[:, 0:KD, ds(c * P, P)], yssm[:, :, :]).then_inc(ys_kept, 16)
            for batch in range(2):
                after(act, vn_done, c * 2 + (batch + 1))
                after(act, o_done, c * 2)
                a(vnew[:, heads_of(batch), :].rearrange("p h t -> p (h t)"), bank(4 + batch), ACT.Copy).then_inc(vn_copied, 1)
            out_store(c)
            act.dma_start(gt[:, :, :], spill_c[:, J_GATE:J_GATE + GATE_T, ds(c * P, P)]).then_inc(in_g, 16)
        out_squares(NCH)
        out_ln(NCH)
        out_exp(NCH)
        out_store(NCH)

    def dve_masks(dve):
        v, step = nc.vector, [0]

        def then(ins):
            ins.then_inc(mask_step, 1)
            step[0] += 1
            dve.wait_ge(mask_step, step[0])

        o = osq[:, :, :].bitcast(i32)
        dve.wait_ge(iota_done, 2)
        then(v.tensor_tensor(o[:, 2, :], o[:, 0, :], o[:, 1, :], ALU.is_gt))
        then(v.tensor_tensor(o[:, 3, :], o[:, 1, :], o[:, 0, :], ALU.is_gt))
        then(v.tensor_tensor(o[:, 4, :], o[:, 0, :], o[:, 1, :], ALU.bitwise_xor))
        for lv in range(N_LEVEL):
            then(v.tensor_scalar(o[:, 5, :], o[:, 4, :], lv, None, ALU.logical_shift_right))
            then(v.tensor_scalar(o[:, 5, :], o[:, 5, :], 1, None, ALU.is_equal))
            then(v.tensor_tensor(lmask[:, lv, :], o[:, 5, :], o[:, 2, :], ALU.mult))
            then(v.tensor_tensor(lmask_t[:, lv, :], o[:, 5, :], o[:, 3, :], ALU.mult))

    def dve_mixer(dve):
        v = nc.vector
        ready_to_mix(dve)
        dve_masks(dve)
        v.memset(qs[:, :, :], 0.0).then_inc(out_zero, 1)
        v.memset(gt[:, :, :], 0.0).then_inc(out_zero, 1)
        dve.wait_ge(out_zero, 2)
        give(dve, "dve")

        def out_sums(n):
            after(dve, osq_done, n + 1)
            v.reduce_sum(orst[:, :], osq[:, :, :], mybir.AxisListType.X).then_inc(o_ssq, 1)

        def out_scale(n):
            after(dve, orst_done, n * 2 + 2)
            v.tensor_tensor(qs[:, :, :], qs[:, :, :], wide(orst[:, :], P), ALU.mult).then_inc(o_normed, 1)

        def out_gate(n):
            after(dve, ot_done, n + 1)
            after(dve, in_g, n * 16)
            after(dve, yg_kept, n * 16)
            v.scalar_tensor_tensor(out=ygdn[:, :, :], in0=bank(6, 2).rearrange("p (h d) -> p h d", h=8), scalar=pcol("gdn_norm_g"),
                                   in1=gt[:, :, :], op0=ALU.mult, op1=ALU.mult).then_inc(yg_out, 1)

        with dve.Fori(0, NCH) as c:
            def ssm_cols(i):
                return cs[:, i, ROW_DT:ROW_DT + SSM_HEADS]

            def gdn_cols(i, row=ROW_A, batch=None):
                h = slice(0, GDN_HEADS) if batch is None else heads_of(batch)
                return cs[:, i, row + h.start:row + h.stop]

            def hd(ap, h=SSM_HEADS):
                return ap.rearrange("p (h d) -> p h d", h=h)

            after(dve, s_gdn_dec, c * 2)
            v.tensor_copy(cs[:, :, :], tmh[:, ds(c, 1), :, :].rearrange("p o a r -> p (o a) r")).then_inc(cs_ready, 1)
            after(dve, cs_ready, c + 1)
            after(dve, xt_done, c + 1)
            after(dve, diag_done, c * 2)
            after(dve, xcd_ready, c)
            v.tensor_tensor(xc[:, :, :], hd(bank(4, 2)), wide(ssm_cols(TM_DT), SSM_HEAD_DIM), ALU.mult).then_inc(x_scaled, 1)
            after(dve, dec_exp, c * 3 + 1)
            after(dve, sc_done, c + 1)
            for g in range(SSM_GROUPS):
                s = bank(7)[:, g * P:(g + 1) * P].unsqueeze(1).broadcast_to([P, HPG, P])
                v.tensor_tensor(dec[:, g * HPG:(g + 1) * HPG, :], dec[:, g * HPG:(g + 1) * HPG, :], s, ALU.mult).then_inc(m_ready, 1)
            after(dve, qk_rs, c * 4 + 3)
            after(dve, qs_done, c * 2)
            v.tensor_tensor(qkn[:, 8:16, :], qkv[:, 8:16, :], sqn[:, 8:16, :], ALU.mult).then_inc(qk_normed, 1)
            after(dve, vt_done, c + 1)
            v.tensor_tensor(bv[:, :, :], hd(bank(4, 2), 8), wide(gdn_cols(TM_BETA, ROW_U), P), ALU.mult).then_inc(v_scaled, 1)
            after(dve, off_done, c + 1)
            after(dve, yt_done, c)
            v.tensor_tensor(hd(ysum[:, :]), hd(bank(0, 2)), wide(ssm_cols(TM_EXP), SSM_HEAD_DIM), ALU.mult).then_inc(y_sum, 1)
            after(dve, qk_rs, c * 4 + 4)
            v.scalar_tensor_tensor(out=qkn[:, 0:8, :], in0=qkv[:, 0:8, :], scalar=GDN_DK ** -0.5, in1=sqn[:, 0:8, :],
                                   op0=ALU.mult, op1=ALU.mult).then_inc(qk_normed, 1)

            def add_diag(g):
                after(dve, diag_done, c * 2 + (g + 1))
                own = bank(2, 2).rearrange("p (q b d) -> p q b d", q=HPG // 2, b=4)[:, :, 0:4:3, :]
                yg = ysum[:, g * 512:g * 512 + 512].rearrange("p (q b d) -> p q b d", q=HPG // 2, b=2)
                v.tensor_tensor(yg, own, yg, ALU.add).then_inc(y_sum, 1)

            after(dve, y_sum, c * 3 + 1)
            add_diag(0)
            after(dve, kt_done, c + 1)
            v.tensor_tensor(kdec[:, :, :], hd(bank(4, 2), 8), wide(gdn_cols(TM_WD), P), ALU.mult).then_inc(k_scaled, 1)

            def gram_of(batch, which):
                return bank(2 + 2 * batch, 2).rearrange("p (h a t) -> p h a t", h=HA, a=2)[:, :, which, :]

            def q_scores(batch):
                d = dec[:, 16 + batch * HA:16 + batch * HA + HA, :]
                v.tensor_tensor(d, gram_of(batch, 0), d, ALU.mult).then_inc(gram_done, 1)

            after(dve, dec_exp, c * 3 + 2)
            for batch in range(2):
                after(dve, gram_mm, c * 2 + (batch + 1))
                d = dec[:, 24 + batch * HA:24 + batch * HA + HA, :]
                v.scalar_tensor_tensor(out=d, in0=gram_of(batch, 1), scalar=-1.0, in1=d, op0=ALU.mult, op1=ALU.mult).then_inc(gram_done, 1)
            after(dve, dec_exp, c * 3 + 3)
            q_scores(0)
            after(dve, inv_init, c * 2 + 2)
            after(dve, gram_done, c * 4 + 2)

            def fill(dst, mask, data, lv, batch):
                h = heads_of(batch)
                waits_met(dve, dve_met)
                v.copy_predicated(dst[:, h, :], mask[:, lv, :].unsqueeze(1).broadcast_to([P, HA, P]), data).then_inc(inv_step, 1)

            for batch in range(2):
                after(dve, nt_done, c * 2 + (batch + 1))
                fill(inv, lmask, hd(bank(6 + batch), HA), 0, batch)
                fill(inv_t, lmask_t, dec[:, 24 + batch * HA:24 + batch * HA + HA, :], 0, batch)
            q_scores(1)
            add_diag(1)
            after(dve, st_done, c + 1)
            after(dve, s_ssm_dec, c + 1)
            v.tensor_tensor(s_ssm[:, :, :], hd(bank(6, 2)), s_ssm[:, :, :], ALU.add).then_inc(s_ssm_new, 1)
            for lv in range(1, N_LEVEL):
                for batch in range(2):
                    base = 4 * (lv - 1) + 2 * batch if lv < N_LEVEL - 1 else 4 * (lv - 1) + batch - 1
                    after(dve, inv_step, c * N_INV + (4 * (lv - 1) + 2 * batch + 2))
                    if lv < N_LEVEL - 1:
                        after(dve, upd_mm, c * N_UPD + (base + 1))
                        fill(inv, lmask, hd(bank(2 + batch), HA), lv, batch)
                    after(dve, upd_mm, c * N_UPD + (base + 2))
                    fill(inv_t, lmask_t, hd(bank(4 + batch), HA), lv, batch)
                if lv == 1:
                    after(dve, yt_done, c + 1)
                    after(dve, xd_ready, c + 1)
                    after(dve, ys_kept, c * 16)
                    v.tensor_tensor(yssm[:, :, :], hd(bank(6, 2), 8), xd[:, :, :], ALU.add).then_inc(y_mid, 1)
                    after(dve, y_mid, c * 2 + 1)
                    after(dve, in_z, c * 16 + 16)
                    v.tensor_tensor(yssm[:, :, :], yssm[:, :, :], zt[:, :, :], ALU.mult).then_inc(y_mid, 1)
                if lv == 3:
                    out_sums(c)
                if lv == 4:
                    after(dve, yrs_done, c * 2 + 2)
                    for_g = yssm[:, :, :].rearrange("p (g k) t -> p g k t", g=SSM_GROUPS)
                    rs_g = yrs[:, :, :].unsqueeze(2).broadcast_to([P, SSM_GROUPS, 4, P])
                    v.tensor_tensor(for_g, for_g, rs_g, ALU.mult).then_inc(y_out, 1)
                    out_scale(c)
                if lv == 5:
                    out_gate(c)
            for batch in range(2):
                h = heads_of(batch)
                after(dve, ks_done, c * 2 + (batch + 1))
                after(dve, vn_done, c * 2)
                v.tensor_tensor(rhs[:, h, :], hd(bank(batch), HA), wide(gdn_cols(TM_EXP, ROW_U, batch), P), ALU.mult).then_inc(r_step, 1)
                after(dve, r_step, c * 4 + (2 * batch + 1))
                v.tensor_tensor(rhs[:, h, :], bv[:, h, :], rhs[:, h, :], ALU.subtract).then_inc(r_step, 1)
            for batch in range(2):
                h = heads_of(batch)
                after(dve, qs_done, c * 2 + (batch + 1))
                v.tensor_tensor(qs[:, h, :], hd(bank(2 + batch), HA), wide(gdn_cols(TM_EXP, ROW_A, batch), P), ALU.mult).then_inc(qs_scaled, 1)
            after(dve, qs_scaled, c * 2 + 2)
            for batch in range(2):
                h = heads_of(batch)
                after(dve, ds_done, c * 2 + (batch + 1))
                after(dve, s_gdn_dec, c * 2 + (batch + 1))
                v.tensor_tensor(s_gdn[:, h, :], hd(bank(batch), HA), s_gdn[:, h, :], ALU.add).then_inc(s_gdn_new, 1)
                after(dve, o_done, c * 2 + (batch + 1))
                v.tensor_tensor(qs[:, h, :], hd(bank(6 + batch), HA), qs[:, h, :], ALU.add).then_inc(o_sum, 1)
        out_sums(NCH)
        out_scale(NCH)
        out_gate(NCH)

    U_BRG, U_WO, U_FFN = U_BRS + 8, U_BRS + 16, U_BRS + 24
    Q_BRS = 1 + N_SPILL // 2
    Q_FFN = Q_BRS + 12
    O_BRG, O_WO = O_BRS + 8, O_BRS + 16
    O_N1 = O_WO + 8
    O_N2 = O_N1 + 1
    O_FFN = O_N2 + 1
    FFN_ITERS = (FFN_GROUPS - 2) // 2
    GU_U, DN_U, GU_Q, DN_Q, GU_O, DN_O = 4, 2, 2, 1, 4, 8
    U_LOOP, Q_LOOP, O_LOOP = U_FFN + 2 * GU_U + DN_U, Q_FFN + 2 * GU_Q + DN_Q, O_FFN + 2 * GU_O + DN_O
    PU, PQ, PO = 2 * (GU_U + DN_U), 2 * (GU_Q + DN_Q), 2 * (GU_O + DN_O)
    U_LAST, Q_LAST, O_LAST = U_LOOP + FFN_ITERS * PU, Q_LOOP + FFN_ITERS * PQ, O_LOOP + FFN_ITERS * PO
    O_N3 = O_LAST + DN_O
    U_PP, Q_PP, O_PP = U_LAST + DN_U, Q_LAST + DN_Q, O_N3 + 1
    U_PG, Q_PG, O_PG = U_PP + 2, Q_PP + 1, O_PP + 8
    O_N4 = O_PG + 8
    O_OUT = O_N4 + 1

    def at_it(it, per, const):
        return const if it is None else it * per + const

    def ffn_steps(eng, gate_up, down):
        gate_up(None, 0, U_FFN, Q_FFN, O_FFN)
        gate_up(None, 1, U_FFN + GU_U, Q_FFN + GU_Q, O_FFN + GU_O)
        down(None, 0, U_FFN + 2 * GU_U, Q_FFN + 2 * GU_Q, O_FFN + 2 * GU_O)
        with eng.Fori(0, FFN_ITERS) as it:
            for i in range(2):
                u, q, o = U_LOOP + i * PU // 2, Q_LOOP + i * PQ // 2, O_LOOP + i * PO // 2
                gate_up(it, 2 + i, u, q, o)
                down(it, 1 + i, u + GU_U, q + GU_Q, o + GU_O)

    branch_blocks = [branch_weights(w, n) for w in range(2) for n in range(4)] + \
        [weights_k(w_out)[:, :, n * 256:(n + 1) * 256] for n in range(4)]
    w_gate_k, w_up_k, w_pg_k = weights_k(w_ffn_gate), weights_k(w_ffn_up), weights_k(w_ple_gate)
    w_down_k = w_ffn_down.rearrange("l (g k q) n -> g q (l k) n", k=2, q=P)
    w_pp_k = weights_k(w_ple_proj)
    L_Y, L_MIX, L_FFN, L_X2 = KD, 3 * KD, 4 * KD, 5 * KD

    def sp_tail(sp):
        blocks = [2]

        def next_block():
            if blocks[0] < len(branch_blocks):
                load_block(sp, branch_blocks[blocks[0]], Q_BRS, blocks[0])
                blocks[0] += 1

        after(sp, ys_kept, 16 * NCH)
        after(sp, yg_kept, 16 * (NCH + 1))
        for which in range(2):
            for k in range(KD):
                i = which * KD + k
                if k >= 2 or which:
                    sp.wait_ge(lo_done, L_Y + i - 1)
                sp.dma_start(ring3[:, k % 2, :], y_cm[i][:, P * which:P * which + SEQ]).then_inc(y_in[k % 2], 16)
            for j in range(8):
                i = which * 8 + j
                if j % 2 == 0:
                    next_block()
                if i >= 2:
                    sp.wait_ge(gated, i - 1)
                sp.dma_start(mg3[:, j % 2, :], spill[J_MG + i]).then_inc(mg_in[j % 2], 16)
        while blocks[0] < len(branch_blocks):
            next_block()

        def gu_load(it, g, u, q, o):
            for i, w in enumerate((w_gate_k, w_up_k)):
                c0 = 256 * g
                src = w[:, :, c0:c0 + 256] if it is None else w[:, :, ds(it * 512 + c0, 256)]
                load_block(sp, src, q, i, it, PQ)
            if it is None and g == 0:
                for k in range(KD):
                    if k >= 2:
                        sp.wait_ge(x1_step, 2 * (k - 1))
                    sp.dma_start(res3[:, k % 2, :], x_cm[k]).then_inc(res_in[k % 2], 16)

        def dn_load(it, g, u, q, o):
            src = w_down_k[g] if it is None else w_down_k[ds(it * 2 + g, 1)].rearrange("g q k n -> (g q) k n")
            load_block(sp, src, q, 0, it, PQ)

        ffn_steps(sp, gu_load, dn_load)
        sp.dma_start(res4[:, :, :], p_cm.rearrange("k q t -> q k t")).then_inc(p4_in, 16)
        dn_load(None, FFN_GROUPS - 1, U_LAST, Q_LAST, O_LAST)
        load_block(sp, w_pp_k, Q_PP, 0)
        for k in range(KD):
            sp.wait_ge(p_lo_done, 2)
            sp.wait_ge(x1_kept, 16)
            if k >= 2:
                sp.wait_ge(x2_step, 2 * (k - 1))
            sp.dma_start(res4[:, k % 2, :], x1_cm[k]).then_inc(res4_in[k % 2], 16)
        for n in range(4):
            load_block(sp, w_pg_k[:, :, n * 256:(n + 1) * 256], Q_PG, n)
        for t in range(NCH):
            b, c = uses(O_OUT, t)
            sp.wait_ge(tile_free[b], c + 1)
            sp.dma_start(out_rows[t], ring3[:, t % 2, :]).then_inc(out_kept[t % 2], 16)
        for i in range(2):
            sp.wait_ge(out_kept[i], 16 * (NCH // 2))
        sp.wait_ge(xt_kept, 16)
        sp.wait_ge(pt_kept, 16)

    def pool_tail(pool):
        for n in range(1, 24):
            split_unit(pool, U_BRS, n)

        def gu_split(it, g, u, q, o):
            for n in range(GU_U):
                split_unit(pool, u, n, it, PU)

        def dn_split(it, g, u, q, o):
            for n in range(DN_U):
                split_unit(pool, u, n, it, PU, k=2)

        ffn_steps(pool, gu_split, dn_split)
        dn_split(None, FFN_GROUPS - 1, U_LAST, Q_LAST, O_LAST)
        for n in range(2):
            split_unit(pool, U_PP, n, k=2)
        for n in range(8):
            split_unit(pool, U_PG, n)

    def pe_sum(pe, o, acc, nth):
        b = wait_buffer(pe, o)
        pe.wait_ge(acc_done, KD * (nth + 1))
        for half in range(2):
            last = nc.tensor.matmul(ps[:, 2 * b + half, :], ones[:, :], acc[:, half * 512:half * 512 + 512], start=True, stop=True)
        last.then_inc(tile_done[b], 1)

    def pe_short(pe, u, o, it, pu, po, mov_hi, mov_lo):
        slot = u % 2
        pe.wait_ge(split_done, at_it(it, 2 * pu, 2 * u + 2))
        wh, wl = (w[:, slot, :].rearrange("p (k n) -> p k n", k=2) for w in (w_hi, w_lo))
        for n in range(4):
            b = wait_buffer(pe, o, n, it, po)
            for k in range(2):
                for half in range(2):
                    dst = ps[:, 2 * b + half, :]
                    c = slice(half * 512, half * 512 + 512)
                    first = nc.tensor.matmul(dst, wh[:, k, n * P:(n + 1) * P], mov_hi[:, k, c], start=(k == 0), stop=False)
                    if n == 0 and k == 0 and half == 0:
                        first.then_inc(unit_begun, 1)
                    nc.tensor.matmul(dst, wh[:, k, n * P:(n + 1) * P], mov_lo[:, k, c], start=False, stop=False)
                    last = nc.tensor.matmul(dst, wl[:, k, n * P:(n + 1) * P], mov_hi[:, k, c], start=False, stop=(k == 1))
            last.then_inc(tile_done[b], 1)

    def pe_tail(pe):
        mov = (act_hi3, act_lo3)
        for u0, o0, base in ((U_BRS, O_BRS, L_Y), (U_BRG, O_BRG, L_Y + KD), (U_WO, O_WO, L_MIX)):
            with pe.Fori(0, 2) as it:
                for n in range(4):
                    pe_unit(pe, u0, o0, n, it, 4, mov=mov, ready=(lo_done, base) if n == 0 else None)
        pe_sum(pe, O_N1, acc3, 0)
        pe_norm(pe, O_N2, sq3, 1)

        def gu(it, g, u, q, o):
            for n in range(GU_U):
                first = it is None and g == 0 and n == 0
                pe_unit(pe, u, o, n, it, PU, mov=mov, ready=(lo_done, L_FFN) if first else None, per_o=PO)

        def dn(it, g, u, q, o):
            pe.wait_ge(f_lo_done, at_it(it, 4, 2 * g + 2))
            for n in range(DN_U):
                pe_short(pe, u + n, o + 4 * n, it, PU, PO, f_hi[:, g % 2], f_lo[:, g % 2])

        ffn_steps(pe, gu, dn)
        dn(None, FFN_GROUPS - 1, U_LAST, Q_LAST, O_LAST)
        pe_sum(pe, O_N3, fa[:, 0, :], 1)
        pe.wait_ge(p_lo_done, 2)
        for n in range(2):
            pe_short(pe, U_PP + n, O_PP + 4 * n, None, 0, 0, p_hi4, p_lo4)
        with pe.Fori(0, 2) as it:
            for n in range(4):
                pe_unit(pe, U_PG, O_PG, n, it, 4, mov=mov, ready=(lo_done, L_X2) if n == 0 else None)
        pe_sum(pe, O_N4, fa[:, 0, :], 2)
        pe.wait_ge(fin_step, 2 * KD)
        for t in range(NCH):
            b = wait_buffer(pe, O_OUT, t)
            for k in range(KD):
                last = nc.tensor.transpose(buf(b)[:, k * P:(k + 1) * P], pj[:, k, t * P:(t + 1) * P], ident[:, :])
            last.then_inc(tile_done[b], 1)

    def act_square(act, nth, j, src, ring):
        if j >= 2:
            act.wait_ge(acc_done, KD * nth + j - 1)
        nc.scalar.activation(ring[:, j % 2, :], src, ACT.Square).then_inc(sq_done, 1)

    def act_tail(act):
        a = nc.scalar.activation
        after(act, ys_kept, 16 * NCH)
        after(act, yg_kept, 16 * (NCH + 1))
        for which in range(2):
            if which:
                b = wait_tile(act, O_BRG - 1)
            for k in range(KD):
                act.wait_ge(y_in[k % 2], 16 * (4 * which + k // 2 + 1))
                a(act_hi3[:, k, :], ring3[:, k % 2, :], ACT.Copy, scale=1.0 if which else pcol("ssm_norm_g", k)).then_inc(hi_done, 1)
        b = wait_tile(act, O_WO - 1)
        for k in range(KD):
            act.wait_ge(mixed, KD + k + 1)
            a(act_hi3[:, k, :], tile3[:, k, :], ACT.Copy).then_inc(hi_done, 1)
        for j in range(8):
            b = wait_tile(act, O_WO, j)
            act.wait_ge(lo_done, L_MIX + KD)
            act_square(act, 0, j, buf(b), sq3)
            a(tile3[:, j, :], buf(b), ACT.Copy).then_inc(tile_free[b], 1)
        act_norm_factor(act, O_N1, rs3, 1)
        for k in range(KD):
            if k >= 2:
                act.wait_ge(norm_sum, KD - 1 + k - 1)
            act.wait_ge(x1_step, 2 * k + 2)
            a(sq3[:, k % 2, :], tile3[:, k, :], ACT.Square).then_inc(norm_sq, 1)
        act.dma_start(x1_cm.rearrange("k q t -> q k t"), tile3[:, :, :]).then_inc(x1_kept, 16)
        act_norm_factor(act, O_N2, rs3, 2)
        for k in range(KD):
            act.wait_ge(norm_h, KD + k + 1)
            a(act_hi3[:, k, :], ring3[:, k % 2, :], ACT.Copy).then_inc(hi_done, 1)
        act.wait_ge(lo_done, L_FFN + KD)

        def gu(it, g, u, q, o):
            for i in range(2):
                t = 2 * g + i
                act.wait_ge(fconv, at_it(it, 12, 3 * t + 3))
                a(fa[:, i, :], fa[:, i, :], ACT.Gelu_apprx_tanh).then_inc(gelu_done, 1)
            for i in range(2):
                b, c = uses(o, 2 + i, it, PO)
                act.wait_ge(tile_free[b], c + 1)
                if it is not None or g >= 2:
                    wait_tile(act, o - 1, 0, it, PO)
                a(f_hi[:, g % 2, i, :], ring3[:, i, :], ACT.Copy).then_inc(f_hi_done, 1)

        ffn_steps(act, gu, lambda *_: None)
        act.wait_ge(p4_in, 16)
        for k in range(2):
            a(p_hi4[:, k, :], res4[:, k, :], ACT.Copy).then_inc(p_hi_done, 1)
        act.wait_ge(f_lo_done, D_FF // P)
        for j in range(8):
            b, c = uses(O_LAST, j)
            act.wait_ge(tile_free[b], c + 1)
            act_square(act, 1, j, tile3[:, j, :], ring3)
        act_norm_factor(act, O_N3, fa[:, 1, :], 3)
        for k in range(KD):
            b = wait_tile(act, O_PP, k)
            a(pj[:, k, :], buf(b), ACT.Copy).then_inc(tile_free[b], 1)
            act.wait_ge(x2_step, 2 * k + 2)
            a(act_hi3[:, k, :], tile3[:, k, :], ACT.Copy).then_inc(hi_done, 1)
        for j in range(8):
            if j >= 2:
                act.wait_ge(e_done, j - 1)
            else:
                act.wait_ge(x2_step, 2 * KD)
            b = wait_tile(act, O_PG, j)
            a(res4[:, j % 2, :], buf(b), ACT.Sigmoid).then_inc(tile_free[b], 1)
            if j >= 1:
                act.wait_ge(e_done, j)
                act_square(act, 2, j - 1, pj[:, j - 1, :], ring3)
        act.wait_ge(e_done, 8)
        act_square(act, 2, 7, pj[:, 7, :], ring3)
        act_norm_factor(act, O_N4, fa[:, 1, :], 4)
        for t in range(NCH):
            if t % 2:
                continue
            if t >= 2:
                act.wait_ge(out_kept[t % 2], 16 * (t // 2))
            b = wait_tile(act, O_OUT, t)
            a(ring3[:, t % 2, :], buf(b), ACT.Copy).then_inc(tile_free[b], 1)

    def dve_square_sum(dve, nth, j, ring, acc):
        dve.wait_ge(sq_done, KD * nth + j + 1)
        if j == 0:
            nc.vector.tensor_copy(acc, ring[:, 0, :]).then_inc(acc_done, 1)
        else:
            dve.wait_ge(acc_done, KD * nth + j)
            nc.vector.tensor_tensor(acc, acc, ring[:, j % 2, :], ALU.add).then_inc(acc_done, 1)

    def dve_residual(dve, gname, rs, res, res_sem, step):
        for k in range(KD):
            nc.vector.scalar_tensor_tensor(out=tile3[:, k, :], in0=tile3[:, k, :], scalar=pcol(gname, k), in1=rs,
                                           op0=ALU.mult, op1=ALU.mult).then_inc(step, 1)
            dve.wait_ge(step, 2 * k + 1)
            dve.wait_ge(res_sem[k % 2], 16 * (k // 2 + 1))
            nc.vector.tensor_tensor(tile3[:, k, :], tile3[:, k, :], res[:, k % 2, :], ALU.add).then_inc(step, 1)

    def dve_tail(dve):
        v = nc.vector
        for which in range(2):
            for k in range(KD):
                dve.wait_ge(hi_done, L_Y + KD * which + k + 1)
                hi = act_hi3[:, k, :].bitcast(f32)
                if which:
                    v.tensor_tensor(act_lo3[:, k, :], ring3[:, k % 2, :], hi, ALU.subtract).then_inc(lo_done, 1)
                else:
                    v.scalar_tensor_tensor(out=act_lo3[:, k, :], in0=ring3[:, k % 2, :], scalar=pcol("ssm_norm_g", k), in1=hi,
                                           op0=ALU.mult, op1=ALU.subtract).then_inc(lo_done, 1)
            for j in range(8):
                b = wait_tile(dve, (O_BRS, O_BRG)[which], j)
                dve.wait_ge(mg_in[j % 2], 16 * (4 * which + j // 2 + 1))
                if not which:
                    v.tensor_tensor(tile3[:, j, :], buf(b), mg3[:, j % 2, :], ALU.mult).then_inc(tile_free[b], 1)
                    dve.wait_ge(tile_free[b], uses(O_BRS, j)[1] + 1)
                    nc.vector.sem_inc(gated, 1)
                    nc.vector.sem_inc(mixed, 1)
                else:
                    if j >= 2:
                        dve.wait_ge(mixed, KD + j - 1)
                    v.tensor_tensor(sq3[:, j % 2, :], buf(b), mg3[:, j % 2, :], ALU.mult).then_inc(tile_free[b], 1)
                    dve.wait_ge(tile_free[b], uses(O_BRG, j)[1] + 1)
                    nc.vector.sem_inc(gated, 1)
                    v.tensor_tensor(tile3[:, j, :], tile3[:, j, :], sq3[:, j % 2, :], ALU.add).then_inc(mixed, 1)
        for k in range(KD):
            dve.wait_ge(hi_done, L_MIX + k + 1)
            v.tensor_tensor(act_lo3[:, k, :], tile3[:, k, :], act_hi3[:, k, :].bitcast(f32), ALU.subtract).then_inc(lo_done, 1)
        for j in range(8):
            dve_square_sum(dve, 0, j, sq3, acc3[:, :])
        dve.wait_ge(norm_rs, 2)
        dve.wait_ge(tile_free[uses(O_WO, 7)[0]], uses(O_WO, 7)[1] + 1)
        dve_residual(dve, "g_mix_post", rs3[:, :], res3, res_in, x1_step)
        dve_scale_split(dve, "g_ffn_pre", tile3, ring3, rs3, act_hi3, act_lo3, 2, L_FFN)
        dve.wait_ge(lo_done, L_FFN + KD)
        v.memset(xin3[:, 0:2], 0.0).then_inc(pads_done, 1)
        dve.wait_ge(pads_done, 3)

        def gu(it, g, u, q, o):
            for i in range(2):
                t = 2 * g + i

                def col_of(name, n):
                    return pcol(name, n) if it is None else pcol_at(name, n, it, 4)

                b = wait_tile(dve, o, i, it, PO)
                if it is not None or t > 0:
                    dve.wait_ge(fconv, at_it(it, 12, 3 * t))
                v.tensor_copy(xin3[:, 2:2 + SEQ], buf(b)).then_inc(tile_free[b], 1)
                dve.wait_ge(tile_free[b], uses(o, i, it, PO)[1] + 1)
                v.tensor_scalar(fa[:, i, :], xin3[:, 2:2 + SEQ], col_of("conv_ffn_w", 2 * 32 + t), col_of("conv_ffn_b", t),
                                ALU.mult, ALU.add).then_inc(fconv, 1)
                for tap in (1, 0):
                    dve.wait_ge(fconv, at_it(it, 12, 3 * t + 2 - tap))
                    v.scalar_tensor_tensor(out=fa[:, i, :], in0=xin3[:, tap:tap + SEQ], scalar=col_of("conv_ffn_w", tap * 32 + t),
                                           in1=fa[:, i, :], op0=ALU.mult, op1=ALU.add).then_inc(fconv, 1)
            for i in range(2):
                t = 2 * g + i
                b = wait_tile(dve, o, 2 + i, it, PO)
                dve.wait_ge(gelu_done, at_it(it, 4, t + 1))
                if it is not None or g > 0:
                    dve.wait_ge(f_lo_done, at_it(it, 4, t - 1))
                v.tensor_tensor(ring3[:, i, :], buf(b), fa[:, i, :], ALU.mult).then_inc(tile_free[b], 1)
            for i in range(2):
                t = 2 * g + i
                dve.wait_ge(f_hi_done, at_it(it, 4, t + 1))
                v.tensor_tensor(f_lo[:, g % 2, i, :], ring3[:, i, :], f_hi[:, g % 2, i, :].bitcast(f32), ALU.subtract).then_inc(f_lo_done, 1)

        def dn(it, g, u, q, o):
            for j in range(8):
                b = wait_tile(dve, o, j, it, PO)
                if it is None and g == 0:
                    dve.wait_ge(x1_kept, 16)
                    v.tensor_copy(tile3[:, j, :], buf(b)).then_inc(tile_free[b], 1)
                else:
                    v.tensor_tensor(tile3[:, j, :], buf(b), tile3[:, j, :], ALU.add).then_inc(tile_free[b], 1)

        ffn_steps(dve, gu, dn)
        for k in range(2):
            dve.wait_ge(p_hi_done, k + 1)
            v.tensor_tensor(p_lo4[:, k, :], res4[:, k, :], p_hi4[:, k, :].bitcast(f32), ALU.subtract).then_inc(p_lo_done, 1)
        for j in range(8):
            b = wait_tile(dve, O_LAST, j)
            v.tensor_tensor(tile3[:, j, :], buf(b), tile3[:, j, :], ALU.add).then_inc(tile_free[b], 1)
            if j >= 1:
                dve_square_sum(dve, 1, j - 1, ring3, fa[:, 0, :])
        dve_square_sum(dve, 1, 7, ring3, fa[:, 0, :])
        dve.wait_ge(norm_rs, 4)
        for k in range(KD):
            v.scalar_tensor_tensor(out=tile3[:, k, :], in0=tile3[:, k, :], scalar=pcol("g_ffn_post", k), in1=fa[:, 1, :],
                                   op0=ALU.mult, op1=ALU.mult).then_inc(x2_step, 1)
            dve.wait_ge(x2_step, 2 * k + 1)
            dve.wait_ge(res4_in[k % 2], 16 * (k // 2 + 1))
            v.tensor_tensor(tile3[:, k, :], tile3[:, k, :], res4[:, k % 2, :], ALU.add).then_inc(x2_step, 1)
            if k >= 1:
                dve.wait_ge(hi_done, L_X2 + k)
                v.tensor_tensor(act_lo3[:, k - 1, :], tile3[:, k - 1, :], act_hi3[:, k - 1, :].bitcast(f32), ALU.subtract).then_inc(lo_done, 1)
        dve.wait_ge(hi_done, L_X2 + KD)
        v.tensor_tensor(act_lo3[:, 7, :], tile3[:, 7, :], act_hi3[:, 7, :].bitcast(f32), ALU.subtract).then_inc(lo_done, 1)
        for j in range(8):
            b, c = uses(O_PG, j)
            dve.wait_ge(tile_free[b], c + 1)
            v.tensor_tensor(pj[:, j, :], pj[:, j, :], res4[:, j % 2, :], ALU.mult).then_inc(e_done, 1)
            if j >= 1:
                dve_square_sum(dve, 2, j - 1, ring3, fa[:, 0, :])
        dve_square_sum(dve, 2, 7, ring3, fa[:, 0, :])
        dve.wait_ge(norm_rs, 5)
        for k in range(KD):
            v.scalar_tensor_tensor(out=pj[:, k, :], in0=pj[:, k, :], scalar=pcol("g_ple_post", k), in1=fa[:, 1, :],
                                   op0=ALU.mult, op1=ALU.mult).then_inc(fin_step, 1)
            dve.wait_ge(fin_step, 2 * k + 1)
            v.tensor_tensor(pj[:, k, :], pj[:, k, :], tile3[:, k, :], ALU.add).then_inc(fin_step, 1)
        for t in range(1, NCH, 2):
            if t >= 2:
                dve.wait_ge(out_kept[1], 16 * (t // 2))
            b = wait_tile(dve, O_OUT, t)
            v.tensor_copy(ring3[:, 1, :], buf(b)).then_inc(tile_free[b], 1)

    @block.sync
    def _(sp):
        for t in range(NCH):
            if t >= 2:
                b, c = uses(O_X, t - 2)
                sp.wait_ge(tile_done[b], c + 1)
            sp.dma_start(xrow[:, t % 2, :], x_rows[t]).then_inc(x_in[t % 2], 16)
            if t == 1:
                sp.wait_ge(consts_done, N_CONST)
                small = w_raw[:, 0, :].rearrange("p (k n) -> p k n", k=KD)
                for col, n, row in ((COL_DT, SSM_HEADS, ROW_DT), (COL_A, GDN_HEADS, ROW_A), (COL_A, GDN_HEADS, ROW_U),
                                    (COL_B, GDN_HEADS, ROW_B)):
                    sp.dma_start(small[:, :, row:row + n], w_in_k[:, :, col:col + n]).then_inc(small_in, 16)
                sp.dma_start(prow[:, :, :], p_rows).then_inc(p_in, 16)
        for kind, col, tiles, j0, o0 in PROJ:
            def load(it, n):
                if n % 2 == 0:
                    c0 = col + P * n
                    src = w_in_k[:, :, c0:c0 + 2 * P] if it is None else w_in_k[:, :, ds(it * (4 * P) + c0, 2 * P)]
                    load_block(sp, src, 1 + j0 // 2, n // 2, it, 2)
            run_tiles(sp, tiles, j0, load)
        sp_mixer(sp)
        sp_tail(sp)

    @block.gpsimd
    def _(pool):
        g = nc.gpsimd
        inits = [g.memset(w_raw[:, 0, :], 0.0), g.memset(stage[:, :, :], 0.0), g.memset(hv[:, 0:1], 1.0),
                 g.memset(hv[:, 1:4], 0.0), g.memset(ones[:, :], 1.0), g.memset(ident[:, :], 0.0),
                 g.memset(tri[:, :], 1.0), g.memset(m_incl[:, :], 0.0), g.memset(m_strict[:, :], 0.0),
                 g.memset(eps_t[:, :], EPS)]
        for i in inits:
            i.then_inc(consts_done, 1)
        pool.wait_ge(consts_done, len(inits))
        g.memset(hv[ROW_B:ROW_B + GDN_HEADS, 0:1], -1.0).then_inc(consts_done, 1)
        pool.wait_ge(consts_done, len(inits) + 1)
        for m, op, base, fill in ((ident, ALU.not_equal, 0, 1.0), (tri, ALU.is_ge, 0, 0.0), (m_incl, ALU.is_ge, 0, -BIG),
                                  (m_strict, ALU.is_gt, 0, -BIG)):
            g.affine_select(out=m[:, :], in_=m[:, :], compare_op=op, fill=fill, base=base, pattern=[[1, P]],
                            channel_multiplier=-1).then_inc(consts_done, 1)
        assert len(inits) + 5 == N_CONST
        split_unit(pool, U_SMALL, 0)
        for kind, col, tiles, j0, o0 in PROJ:
            run_tiles(pool, tiles, j0, lambda it, n: split_unit(pool, 1 + j0, n, it, 4))
        pool_mixer(pool)
        pool_tail(pool)

    @block.tensor
    def _(pe):
        pe.wait_ge(consts_done, N_CONST)
        pe.wait_ge(params_in, N_PARAM_DMA * 16)
        b = wait_buffer(pe, O_PAR)
        for a in range(4):
            last = nc.tensor.transpose(buf(b)[:, a * P:(a + 1) * P], stage[:, a, :], ident[:, :])
        last.then_inc(tile_done[b], 1)
        for t in range(NCH):
            pe.wait_ge(x_in[t % 2], 16 * (t // 2 + 1))
            b = wait_buffer(pe, O_X, t)
            for k in range(KD):
                last = nc.tensor.transpose(buf(b)[:, k * P:(k + 1) * P], xrow[:, t % 2, k * P:(k + 1) * P], ident[:, :])
            last.then_inc(tile_done[b], 1)
        pe.wait_ge(p_in, 16)
        for k in range(2):
            b = wait_buffer(pe, O_P, k)
            for t in range(NCH):
                last = nc.tensor.transpose(buf(b)[:, t * P:(t + 1) * P], prow[:, t, k * P:(k + 1) * P], ident[:, :])
            last.then_inc(tile_done[b], 1)
        pe_norm(pe, O_NORM0, ring_a, 0)
        mov = (act_hi, act_lo)
        pe_unit(pe, U_SMALL, O_SMALL, 0, mov=mov, ready=(lo_done, 0))
        for kind, col, tiles, j0, o0 in PROJ:
            run_tiles(pe, tiles, j0, lambda it, n: pe_unit(pe, 1 + j0, o0, n, it, 4, mov=mov))
            if kind == "gdn":
                for i, (row, step) in enumerate(((1, HEAD_SP), (2, HEAD_L))):
                    pe.wait_ge(head_dve, step)
                    b = wait_buffer(pe, O_TM, i)
                    for c in range(NCH):
                        last = nc.tensor.transpose(buf(b)[:, c * P:(c + 1) * P], hrow[:, row, c * P:(c + 1) * P], ident[:, :])
                    last.then_inc(tile_done[b], 1)
            if j0 == J_Z:
                pe.wait_ge(tm_dve, TM_SRC)
                lg, lb = hrow[:, 0, :], hrow[:, 3, :]
                b = wait_buffer(pe, O_CUM, 0)
                for half in range(2):
                    c = slice(half * 512, half * 512 + 512)
                    nc.tensor.matmul(ps[:, 2 * b + half, :], tri[:, :], lg[:, c], start=True, stop=False)
                    last = nc.tensor.matmul(ps[:, 2 * b + half, :], ident[:, :], lb[:, c], start=False, stop=True)
                last.then_inc(tile_done[b], 1)
                b = wait_buffer(pe, O_CUM, 1)
                for ch in range(NCH):
                    c = slice(ch * P, ch * P + P)
                    nc.tensor.matmul(buf(b)[:, c], lg[:, c], tri[:, :], start=True, stop=False)
                    last = nc.tensor.matmul(buf(b)[:, c], lb[:, c], ident[:, :], start=False, stop=True)
                last.then_inc(tile_done[b], 1)
                b = wait_buffer(pe, O_CUM, 2)
                for half in range(2):
                    c = slice(half * 512, half * 512 + 512)
                    last = nc.tensor.matmul(ps[:, 2 * b + half, :], ones[:, :], lg[:, c], start=True, stop=True)
                last.then_inc(tile_done[b], 1)
        pe_mixer(pe)
        pe_tail(pe)

    @block.scalar
    def _(act):
        act.wait_ge(consts_done, N_CONST)
        rows = [("g_mix_pre", g_mix_pre), ("g_mix_post", g_mix_post), ("g_ffn_pre", g_ffn_pre),
                ("g_ffn_post", g_ffn_post), ("g_ple_post", g_ple_post), ("ssm_norm_g", ssm_norm_g),
                ("gdn_norm_g", gdn_norm_g), ("conv_ssm_b", conv_ssm_b), ("conv_ffn_b", conv_ffn_b)]
        for name, v in rows:
            n = v.shape[1] // P
            act.dma_start(stage[PR[name]:PR[name] + n, 0, :], v.rearrange("o (r q) -> (o r) q", q=P)).then_inc(params_in, 16)
        for i, w in enumerate((conv_ssm_w, conv_gdn_w, conv_ffn_w)):
            n = w.shape[1] * w.shape[2] // P
            act.dma_start(stage[0:n, i + 1, :], w.rearrange("o t (r q) -> (o t r) q", q=P)).then_inc(params_in, 16)
        for half in range(2):
            v = ssm_d.rearrange("o (k two) -> two (o k)", two=2)[half:half + 1, :]
            act.dma_start(d_ch[64 * half:64 * half + 64, :], v.broadcast_to([64, KD]), allow_slow_non_contiguous=True).then_inc(params_in, 16)
        for row, n, bias, a_log in ((ROW_DT, SSM_HEADS, ssm_dt_bias, ssm_a_log), (ROW_A, GDN_HEADS, gdn_dt_bias, gdn_a_log),
                                    (ROW_U, GDN_HEADS, gdn_dt_bias, gdn_a_log)):
            act.dma_start(hv[row:row + n, 1:2], bias.rearrange("o h -> h o"), allow_slow_non_contiguous=True).then_inc(hv_in, 16)
            act.dma_start(hv[row:row + n, 2:3], a_log.rearrange("o h -> h o"), allow_slow_non_contiguous=True).then_inc(hv_in, 16)
        act.wait_ge(hv_in, 6 * 16)
        nc.scalar.activation(hv[:, 3:4], hv[:, 2:3], ACT.Exp).then_inc(hv_done, 1)
        for t in range(NCH):
            b = wait_tile(act, O_X, t)
            nc.scalar.activation(tile_f[:, :, t * P:(t + 1) * P], buf(b).rearrange("p (k t) -> p k t", k=KD),
                                 ACT.Copy).then_inc(tile_free[b], 1)
        for t in range(NCH - NBUF, NCH):
            b, c = uses(O_X, t)
            act.wait_ge(tile_free[b], c + 1)
        act.dma_start(x_cm.rearrange("k q t -> q k t"), tile_f[:, :, :]).then_inc(xt_kept, 16)
        for k in range(2):
            b = wait_tile(act, O_P, k)
            nc.scalar.activation(ring_b[:, k, :], buf(b), ACT.Copy).then_inc(tile_free[b], 1)
        for k in range(2):
            b, c = uses(O_P, k)
            act.wait_ge(tile_free[b], c + 1)
        act.dma_start(p_cm.rearrange("k q t -> q k t"), ring_b[:, :, :]).then_inc(pt_kept, 16)
        act_norm(act, O_NORM0, tile_f, ring_a, rstd, 0)
        for k in range(KD):
            act.wait_ge(norm_h, k + 1)
            nc.scalar.activation(act_hi[:, k, :], ring_b[:, k % 2, :], ACT.Copy).then_inc(hi_done, 1)
        def head_rows():
            b = wait_tile(act, O_SMALL)
            act.wait_ge(lo_done, KD)
            act.wait_ge(xt_kept, 16)
            nc.scalar.activation(hrow[:, 0, :], buf(b), ACT.Identity, scale=hv[:, 0:1], bias=hv[:, 1:2]).then_inc(tile_free[b], 1)
            act.wait_ge(tile_free[b], uses(O_SMALL, 0)[1] + 1)
            nc.scalar.activation(hrow[:, 1, :], hrow[:, 0, :], ACT.Abs).then_inc(head_act, 1)
            act.wait_ge(head_act, 1)
            nc.scalar.activation(hrow[:, 1, :], hrow[:, 1, :], ACT.Exp, scale=-1.0).then_inc(head_act, 1)
        head_rows()
        for kind, col, tiles, j0, o0 in PROJ:
            def evict(it, n):
                j = j0 + n
                slot = j % 2
                if it is None:
                    if j >= 2:
                        act.wait_ge(spilled[slot], 16 * (j // 2))
                    else:
                        act.wait_ge(lo_done, KD)
                else:
                    act.wait_ge(spilled[slot], it * 32 + 16 * (j // 2))
                if kind in ("ssm", "gdn"):
                    act.wait_ge(conv_step, 4 * (j + 1) if it is None else it * 16 + 4 * (j + 1))
                    nc.scalar.activation(ring_b[:, slot, :], ring_a[:, slot, :], ACT.Silu).then_inc(conv_out, 1)
                    act.wait_ge(conv_out, j + 1 if it is None else it * 4 + (j + 1))
                else:
                    b = wait_tile(act, o0, n, it, 4)
                    f = ACT.Silu if kind == "silu" else ACT.Sigmoid
                    nc.scalar.activation(ring_b[:, slot, :], buf(b), f).then_inc(tile_free[b], 1)
                    act.wait_ge(tile_free[b], uses(o0, n, it, 4)[1] + 1)
                dst = spill[j] if it is None else spill[ds(it * 4 + j, 1)].rearrange("o q t -> (o q) t")
                act.dma_start(dst, ring_b[:, slot, :]).then_inc(spilled[slot], 16)
            run_tiles(act, tiles, j0, evict)
            if j0 == J_GATE:
                act.wait_ge(tm_dve, TM_END)
                lb = hrow[:, 3, :].rearrange("p (c r) -> p c r", c=NCH)
                nc.scalar.activation(tmh[:, :, TM_BETA, :], lb, ACT.Exp).then_inc(tm_act, 1)
                nc.scalar.activation(tmh[:, :, TM_EXP, :], tmh[:, :, TM_CUM, :], ACT.Exp).then_inc(tm_act, 1)
                nc.scalar.activation(tmh[:, :, TM_WD, :], tmh[:, :, TM_WD, :], ACT.Exp).then_inc(tm_act, 1)
                last = hrow[:, 2, :].rearrange("p (c r) -> p c r", c=NCH)
                nc.scalar.activation(tmh[:, :, TM_LAST, :], last, ACT.Exp).then_inc(tm_act, 1)
                act.dma_start(cum_rows, hrow[:, 1, :]).then_inc(cum_kept, 16)
        act_mixer(act)
        act_tail(act)

    @block.vector
    def _(dve):
        v = nc.vector
        b = wait_tile(dve, O_PAR)
        v.tensor_copy(par_f, buf(b)[:, 0:512]).then_inc(tile_free[b], 1)
        dve.wait_ge(tile_free[b], 1)
        dve.wait_ge(params_in, N_PARAM_DMA * 16)
        dve.wait_ge(hv_done, 1)
        v.tensor_scalar(hv[:, 3:4], hv[:, 3:4], -1.0, None, ALU.mult).then_inc(hv_done, 1)
        dve.wait_ge(pt_kept, 16)
        dve_scale_split(dve, "g_mix_pre", tile_f, ring_b, rstd, act_hi, act_lo, 0, 0)
        for i in range(2):
            dve.wait_ge(lo_done, KD)
            dve.wait_ge(xt_kept, 16)
            v.memset(xin[:, i, 0:3], 0.0).then_inc(pads_done, 1)
        dve.wait_ge(pads_done, 2)
        for kind, col, tiles, j0, o0 in PROJ:
            if kind in ("ssm", "gdn"):
                wname, nt, t0 = ("conv_ssm_w", XBC_T, j0) if kind == "ssm" else ("conv_gdn_w", QKV_T, j0 - J_Q)
                def conv(it, n):
                    j = j0 + n
                    slot = j % 2
                    def col_of(name, i):
                        return pcol(name, i) if it is None else pcol_at(name, i, it, 4)
                    b = wait_tile(dve, o0, n, it, 4)
                    v.tensor_copy(xin[:, slot, 3:3 + SEQ], buf(b)).then_inc(tile_free[b], 1)
                    dve.wait_ge(tile_free[b], uses(o0, n, it, 4)[1] + 1)
                    if it is not None or j >= 2:
                        dve.wait_ge(conv_out, j - 1 if it is None else it * 4 + (j - 1))
                    v.tensor_scalar(ring_a[:, slot, :], xin[:, slot, 3:3 + SEQ], col_of(wname, 3 * nt + t0 + n),
                                    col_of("conv_ssm_b", t0 + n) if kind == "ssm" else None,
                                    ALU.mult, *([ALU.add] if kind == "ssm" else [])).then_inc(conv_step, 1)
                    for tap in (2, 1, 0):
                        step = 4 * j + 3 - tap
                        dve.wait_ge(conv_step, step if it is None else it * 16 + step)
                        v.scalar_tensor_tensor(out=ring_a[:, slot, :], in0=xin[:, slot, tap:tap + SEQ],
                                               scalar=col_of(wname, tap * nt + t0 + n), in1=ring_a[:, slot, :],
                                               op0=ALU.mult, op1=ALU.add).then_inc(conv_step, 1)
                run_tiles(dve, tiles, j0, conv)
            if kind == "ssm" and j0 > 0:
                head_softplus(dve)
            if kind == "gdn":
                tm_sources(dve)
            if j0 == J_Z:
                tm_sums(dve)
        dve_mixer(dve)
        dve_tail(dve)

    ctx.close()


_INS = ['x', 'p', 'g_mix_pre', 'w_in', 'conv_ssm_w', 'conv_ssm_b', 'ssm_dt_bias', 'ssm_a_log', 'ssm_d', 'ssm_norm_g',
        'conv_gdn_w', 'gdn_dt_bias', 'gdn_a_log', 'gdn_norm_g', 'w_br_ssm', 'w_br_gdn', 'w_out', 'g_mix_post',
        'g_ffn_pre', 'w_ffn_gate', 'w_ffn_up', 'conv_ffn_w', 'conv_ffn_b', 'w_ffn_down', 'g_ffn_post',
        'w_ple_gate', 'w_ple_proj', 'g_ple_post']


def kernel(**inputs):
    import numpy as _np
    import concourse.bacc as _bacc
    from concourse import mybir as _mybir
    from concourse.bass_utils import run_bass_kernel_spmd as _run

    nc = _bacc.Bacc("TRN2", target_bir_lowering=False, num_devices=1)
    arrays, args = {}, []
    for name in _INS:
        a = _np.ascontiguousarray(inputs[name])
        arrays[f"in_{name}_dram"] = a
        args.append(nc.dram_tensor(f"in_{name}_dram", a.shape, _mybir.dt.from_np(a.dtype), kind="ExternalInput").ap())
    out = nc.dram_tensor("out_0_dram", (1, SEQ, D_MODEL), _mybir.dt.float32, kind="ExternalOutput").ap()
    hybrid_block_kernel(nc, *args, out)
    r = _run(nc, [arrays], core_ids=[0])
    return r.results[0]["out_0_dram"]
```
